# Optimizing a Trainium2 kernel written in Bass

```python
import jax, jax.numpy as jnp
from jax import lax
import numpy as np

D_MODEL = 1024
BATCH = 1
SEQ = 256
DEPTH = 1
DEC_BATCH = 8
DEC_SEQ = 1
PAST_LEN = 1024
PAGE_SIZE = 128

POOL_WINDOWS = (2, 4, 8, 16)
N_POOL_GROUPS = len(POOL_WINDOWS)
POOL_GROUP_DIM = D_MODEL // 8
D_POOL = N_POOL_GROUPS * POOL_GROUP_DIM
POOL_STATE_LEN = max(POOL_WINDOWS) - 1
HEAD_DIM = 64
N_HEADS = D_MODEL // 128
D_ATT = N_HEADS * HEAD_DIM
Q_BLOCK = 128
FORGET_BIAS_INIT = 3.0
N_BRANCHES = 2
D_IN = D_POOL + 3 * D_ATT + N_HEADS + N_BRANCHES * D_MODEL
N_EXPERT_GROUPS = 4
EXPERTS_PER_GROUP = 8
N_EXPERTS = N_EXPERT_GROUPS * EXPERTS_PER_GROUP
TOP_K_IN_GROUP = 2
D_EXPERT = D_MODEL // 2
RMS_EPS = 1e-6

kernel_name = 'hybrid_pool_fox_hmoe_step'

def rmsnorm(x, g):
    xf = x.astype(jnp.float32)
    y = xf * lax.rsqrt(jnp.mean(xf * xf, axis=-1, keepdims=True) + RMS_EPS)
    return (y * g.astype(jnp.float32)).astype(x.dtype)

def split_projection(h, w_in, b_forget):
    z = h @ w_in
    o1 = D_POOL
    o2 = o1 + D_ATT
    o3 = o2 + D_ATT
    o4 = o3 + D_ATT
    o5 = o4 + N_HEADS
    u, q, k, v, f_logit, g_logit = jnp.split(z, [o1, o2, o3, o4, o5], axis=-1)
    head_shape = z.shape[:-1] + (N_HEADS, HEAD_DIM)
    logf = jax.nn.log_sigmoid((f_logit + b_forget).astype(jnp.float32))
    gates = g_logit.reshape(z.shape[:-1] + (N_BRANCHES, D_MODEL))
    return u, q.reshape(head_shape), k.reshape(head_shape), v.reshape(head_shape), logf, gates

def pool_mixer(u, prefix, start_pos, w_pool, pool_scale):
    B, T, _ = u.shape
    P = POOL_STATE_LEN
    ext = jnp.concatenate([prefix.astype(u.dtype), u], axis=1)
    cs = jnp.cumsum(ext.astype(jnp.float32), axis=1)
    cs = jnp.pad(cs, ((0, 0), (1, 0), (0, 0)))
    pos = start_pos + jnp.arange(T)
    uf = u.astype(jnp.float32)
    outs = []
    for g, w in enumerate(POOL_WINDOWS):
        lo, hi = g * POOL_GROUP_DIM, (g + 1) * POOL_GROUP_DIM
        win_sum = cs[:, P + 1:P + 1 + T, lo:hi] - cs[:, P + 1 - w:P + 1 - w + T, lo:hi]
        count = jnp.minimum(pos + 1, w).astype(jnp.float32)
        outs.append(win_sum / count[None, :, None] - uf[..., lo:hi])
    pooled = jnp.stack(outs, axis=2)
    mixed = jnp.einsum('btgc,gcd->btgd', pooled, w_pool.astype(jnp.float32)).reshape(B, T, D_POOL)
    mixed = mixed * pool_scale.astype(jnp.float32)
    return mixed.astype(u.dtype), ext[:, -P:]

def fox_block(q, c_q, q_pos, k, v, c_k, k_pos):
    s = jnp.einsum('bqhd,bkhd->bhqk', q.astype(jnp.float32), k.astype(jnp.float32)) * (HEAD_DIM ** -0.5)
    bias = jnp.transpose(c_q, (0, 2, 1))[:, :, :, None] - jnp.transpose(c_k, (0, 2, 1))[:, :, None, :]
    mask = k_pos[None, :] <= q_pos[:, None]
    s = jnp.where(mask[None, None], s + bias, -jnp.inf)
    p = jax.nn.softmax(s, axis=-1)
    return jnp.einsum('bhqk,bkhd->bqhd', p, v.astype(jnp.float32)).astype(v.dtype)

def fox_prompt(q, k, v, logf):
    B, T, H, Dh = q.shape
    c = jnp.cumsum(logf, axis=1)
    pos = jnp.arange(T)
    nb = T // Q_BLOCK
    qb = q.reshape(B, nb, Q_BLOCK, H, Dh).swapaxes(0, 1)
    cb = c.reshape(B, nb, Q_BLOCK, H).swapaxes(0, 1)
    pb = pos.reshape(nb, Q_BLOCK)
    out = lax.map(lambda a: fox_block(a[0], a[1], a[2], k, v, c, pos), (qb, cb, pb))
    return out.swapaxes(0, 1).reshape(B, T, H, Dh)

def fox_sample(q, k, v, logf, cache_k, cache_v, cache_logf, page_table):
    DB, T, H, Dh = q.shape
    past = page_table.shape[1] * PAGE_SIZE
    k_past = cache_k[page_table].reshape(DB, past, H, Dh)
    v_past = cache_v[page_table].reshape(DB, past, H, Dh)
    lf_past = cache_logf[page_table].reshape(DB, past, H)
    k_all = jnp.concatenate([k_past, k.astype(k_past.dtype)], axis=1)
    v_all = jnp.concatenate([v_past, v.astype(v_past.dtype)], axis=1)
    lf_all = jnp.concatenate([lf_past.astype(jnp.float32), logf], axis=1)
    c = jnp.cumsum(lf_all, axis=1)
    k_pos = jnp.arange(past + T)
    q_pos = past + jnp.arange(T)
    return fox_block(q, c[:, past:], q_pos, k_all, v_all, c, k_pos)

def merge_branches(pool_out, att_out, gate_logits, w_up_pool, w_up_att, w_out):
    B, T = pool_out.shape[:2]
    gates = jax.nn.sigmoid(gate_logits.astype(jnp.float32))
    y = gates[..., 0, :] * (pool_out @ w_up_pool).astype(jnp.float32) \
        + gates[..., 1, :] * (att_out.reshape(B, T, D_ATT) @ w_up_att).astype(jnp.float32)
    return y.astype(pool_out.dtype) @ w_out

def hier_moe(h, w_rg, b_rg, w_re, b_re, w_gate, w_up, w_down):
    B, T, D = h.shape
    N = B * T
    xf = h.reshape(N, D)
    gl = (xf @ w_rg).astype(jnp.float32) + b_rg.astype(jnp.float32)
    gprob = jax.nn.softmax(gl, axis=-1)
    g_idx = jnp.argmax(gl, axis=-1)
    g_w = jnp.take_along_axis(gprob, g_idx[:, None], axis=1)[:, 0]
    el = jnp.einsum('nd,gde->nge', xf, w_re).astype(jnp.float32) + b_re.astype(jnp.float32)
    el_sel = jnp.take_along_axis(el, g_idx[:, None, None], axis=1)[:, 0]
    top_v, top_i = lax.top_k(el_sel, TOP_K_IN_GROUP)
    top_w = jax.nn.softmax(top_v, axis=-1)
    within = jnp.sum(top_w[..., None] * jax.nn.one_hot(top_i, EXPERTS_PER_GROUP, dtype=jnp.float32), axis=1)
    gate = (g_w[:, None, None] * jax.nn.one_hot(g_idx, N_EXPERT_GROUPS, dtype=jnp.float32)[:, :, None]
            * within[:, None, :]).reshape(N, N_EXPERTS)

    def expert_step(acc, p):
        w1, w3, w2, ge = p
        hdn = jax.nn.silu(xf @ w1) * (xf @ w3)
        return acc + ge[:, None] * (hdn @ w2).astype(jnp.float32), None

    acc, _ = lax.scan(expert_step, jnp.zeros((N, D), jnp.float32), (w_gate, w_up, w_down, gate.T))
    return acc.astype(h.dtype).reshape(B, T, D)

def setup_inputs(seed: int = 0) -> dict:
    key = jax.random.key(seed)
    ks = jax.random.split(key, 24)
    n_pages = PAST_LEN // PAGE_SIZE
    n_used = DEC_BATCH * n_pages
    n_phys = n_used + max(n_used // 4, 1)
    nrm = jax.random.normal
    f32 = jnp.float32
    page_table = jax.random.permutation(ks[5], n_phys)[:n_used].reshape(DEC_BATCH, n_pages).astype(jnp.int32)
    return {
        'x_prompt': nrm(ks[0], (BATCH, SEQ, D_MODEL), f32),
        'x_sample': nrm(ks[1], (DEC_BATCH, DEC_SEQ, D_MODEL), f32),
        'cache_k': nrm(ks[2], (DEPTH, n_phys, PAGE_SIZE, N_HEADS, HEAD_DIM), f32),
        'cache_v': nrm(ks[3], (DEPTH, n_phys, PAGE_SIZE, N_HEADS, HEAD_DIM), f32),
        'cache_logf': jax.nn.log_sigmoid(FORGET_BIAS_INIT + 0.5 * nrm(ks[4], (DEPTH, n_phys, PAGE_SIZE, N_HEADS), f32)),
        'state_pool': nrm(ks[6], (DEPTH, DEC_BATCH, POOL_STATE_LEN, D_POOL), f32),
        'page_table': page_table,
        'norm_mix': 1.0 + 0.02 * nrm(ks[7], (DEPTH, D_MODEL), f32),
        'w_in': nrm(ks[8], (DEPTH, D_MODEL, D_IN), f32) * D_MODEL ** -0.5,
        'b_forget': FORGET_BIAS_INIT + 0.1 * nrm(ks[9], (DEPTH, N_HEADS), f32),
        'w_pool': nrm(ks[10], (DEPTH, N_POOL_GROUPS, POOL_GROUP_DIM, POOL_GROUP_DIM), f32) * POOL_GROUP_DIM ** -0.5,
        'pool_scale': 1.0 + 0.1 * nrm(ks[11], (DEPTH, D_POOL), f32),
        'w_up_pool': nrm(ks[12], (DEPTH, D_POOL, D_MODEL), f32) * D_POOL ** -0.5,
        'w_up_att': nrm(ks[13], (DEPTH, D_ATT, D_MODEL), f32) * D_ATT ** -0.5,
        'w_out': nrm(ks[14], (DEPTH, D_MODEL, D_MODEL), f32) * D_MODEL ** -0.5,
        'norm_ffn': 1.0 + 0.02 * nrm(ks[15], (DEPTH, D_MODEL), f32),
        'w_router_group': nrm(ks[16], (DEPTH, D_MODEL, N_EXPERT_GROUPS), f32) * D_MODEL ** -0.5,
        'b_router_group': 0.01 * nrm(ks[17], (DEPTH, N_EXPERT_GROUPS), f32),
        'w_router_expert': nrm(ks[18], (DEPTH, N_EXPERT_GROUPS, D_MODEL, EXPERTS_PER_GROUP), f32) * D_MODEL ** -0.5,
        'b_router_expert': 0.01 * nrm(ks[19], (DEPTH, N_EXPERT_GROUPS, EXPERTS_PER_GROUP), f32),
        'w_gate': nrm(ks[20], (DEPTH, N_EXPERTS, D_MODEL, D_EXPERT), f32) * D_MODEL ** -0.5,
        'w_up': nrm(ks[21], (DEPTH, N_EXPERTS, D_MODEL, D_EXPERT), f32) * D_MODEL ** -0.5,
        'w_down': nrm(ks[22], (DEPTH, N_EXPERTS, D_EXPERT, D_MODEL), f32) * D_EXPERT ** -0.5,
        'norm_final': 1.0 + 0.02 * nrm(ks[23], (D_MODEL,), f32),
    }

def reference(x_prompt, x_sample, cache_k, cache_v, cache_logf, state_pool, page_table,
              norm_mix, w_in, b_forget, w_pool, pool_scale, w_up_pool, w_up_att, w_out,
              norm_ffn, w_router_group, b_router_group, w_router_expert, b_router_expert,
              w_gate, w_up, w_down, norm_final):
    xp, xs = x_prompt, x_sample
    past = page_table.shape[1] * PAGE_SIZE
    kp_l, vp_l, lfp_l, poolp_l = [], [], [], []
    ks_l, vs_l, lfs_l, pools_l = [], [], [], []
    for l in range(DEPTH):
        h = rmsnorm(xp, norm_mix[l])
        u, q, k, v, logf, gl = split_projection(h, w_in[l], b_forget[l])
        zero_prefix = jnp.zeros((u.shape[0], POOL_STATE_LEN, D_POOL), u.dtype)
        pool_out, pool_new = pool_mixer(u, zero_prefix, 0, w_pool[l], pool_scale[l])
        att = fox_prompt(q, k, v, logf)
        xp = xp + merge_branches(pool_out, att, gl, w_up_pool[l], w_up_att[l], w_out[l])
        xp = xp + hier_moe(rmsnorm(xp, norm_ffn[l]), w_router_group[l], b_router_group[l],
                           w_router_expert[l], b_router_expert[l], w_gate[l], w_up[l], w_down[l])
        kp_l.append(k); vp_l.append(v); lfp_l.append(logf); poolp_l.append(pool_new)
        h = rmsnorm(xs, norm_mix[l])
        u, q, k, v, logf, gl = split_projection(h, w_in[l], b_forget[l])
        pool_out, pool_new = pool_mixer(u, state_pool[l], past, w_pool[l], pool_scale[l])
        att = fox_sample(q, k, v, logf, cache_k[l], cache_v[l], cache_logf[l], page_table)
        xs = xs + merge_branches(pool_out, att, gl, w_up_pool[l], w_up_att[l], w_out[l])
        xs = xs + hier_moe(rmsnorm(xs, norm_ffn[l]), w_router_group[l], b_router_group[l],
                           w_router_expert[l], b_router_expert[l], w_gate[l], w_up[l], w_down[l])
        ks_l.append(k); vs_l.append(v); lfs_l.append(logf); pools_l.append(pool_new)
    y_prompt = rmsnorm(xp, norm_final)
    y_sample = rmsnorm(xs, norm_final)
    return (y_prompt, y_sample,
            jnp.stack(kp_l), jnp.stack(vp_l), jnp.stack(lfp_l), jnp.stack(poolp_l),
            jnp.stack(ks_l), jnp.stack(vs_l), jnp.stack(lfs_l), jnp.stack(pools_l))


_drawn_inputs = setup_inputs


def setup_inputs(seed=0):
    import zlib

    import numpy as np

    out = dict(_drawn_inputs(seed))
    spreads = {}
    factors = {'cache_logf': 6.797,
     'b_router_group': 15.108,
     'b_router_expert': 13.207,
     'norm_final': 24.45,
     'norm_mix': 2.864,
     'norm_ffn': 3.51}
    for name, (base, spread) in spreads.items():
        noise = np.random.default_rng([zlib.crc32(name.encode()), seed]).standard_normal(out[name].shape)
        drawn = base * np.exp(spread * noise) if base else spread * noise
        out[name] = __import__('jax').numpy.asarray(drawn.astype(out[name].dtype))
    for name, factor in factors.items():
        out[name] = (out[name] * factor).astype(out[name].dtype)
    return out
```

```python
import numpy as np
import concourse.bass as bass
from concourse import mybir
from contextlib import ExitStack

F32 = mybir.dt.float32
I32 = mybir.dt.int32
ALU = mybir.AluOpType
ACT = mybir.ActivationFunctionType
AX = mybir.AxisListType

P = 128
D = 1024
DK = D // P
SEQ = 256
PB = SEQ // P
NS = 8
TOK = SEQ + NS
TPAD = SEQ + 32
HEADS, HD = 8, 64
DC = HEADS * HD
CC = DC // P
PAGES, ROWS = 8, 128
NPHYS = 80
WINDOWS = (2, 4, 8, 16)
PLEN = 15
GROUPS, PER_GROUP = 4, 8
EXPERTS = GROUPS * PER_GROUP
FE = 512
FC = FE // P
EPS = 1e-6
QSCALE = HD ** -0.5
BIG = 1e30
C_U, C_Q, C_K, C_V = 0, 1, 2, 3
W_FORGET = 4 * DC
W_GATE = W_FORGET + HEADS
NT = 2 * DK
GPS = DC // P

CAP = 32
RANKS = 288
MAXOVER = 2 * TOK // CAP
NONE = 65536
SLOT = 4096
NSLOT = 9
FRONT = 6


def band(w):
    s, t = np.arange(P)[:, None], np.arange(P)[None, :]
    inside = (t >= s) & (t - s < w)
    own = (s == t).astype(np.float64)
    first = inside / np.minimum(t + 1, w) - own
    full = inside / w - own
    before = ((t + P - s) < w)[:, :PLEN] / w
    state = np.zeros((P, NS))
    for b in range(NS):
        for j in range(PLEN - (w - 1), PLEN):
            state[b * PLEN + j, b] = 1 / w
    mine = np.zeros((P, NS))
    mine[:NS] = np.eye(NS) * (1 / w - 1)
    return first, full, before, state, mine


def constants():
    s, t = np.arange(P)[:, None], np.arange(P)[None, :]
    p = np.arange(P)
    sum8 = np.zeros((P, NS))
    for g in range(4):
        sum8[32 * g:32 * g + NS] = np.eye(NS)
    early = {
        "ident": np.eye(P),
        "sum8": sum8,
        "eps": np.full((P, 1), EPS),
    }
    mask = np.zeros((P, 2 * P))
    mask[:, P:] = np.where(t <= s, 0.0, -BIG)
    other = np.zeros((P, NS))
    other[:NS] = np.where(np.eye(NS) > 0, 0.0, -BIG)
    valid = np.ones((P, 3))
    valid[NS:, 2] = 0
    token = (np.arange(3)[None, :, None] * P + p[:, None, None]) + np.zeros((1, 1, 2))
    pay = np.stack([token, 2 * token + np.arange(2)[None, None, :]], -1)
    late = {
        "later": (s > t),
        "earlier": (s < t),
        "ones": np.ones((P, P)),
        "mask": mask,
        "other": other,
        "valid": valid,
        "first": np.tile(np.arange(EXPERTS, 0, -1.0), (P, 1)),
        "expert": np.tile(np.arange(EXPERTS) * 1.0, (P, 1)),
        "block": np.tile(np.arange(1, 9) * float(CAP), (P, 1)),
        "group": (p // 32)[:, None] * 1.0,
        "part": p[:, None] * 1.0,
        "slots": np.tile(np.arange(CAP) * 1.0, (P, 1)),
        "group4": (p // 32)[:, None] + 4.0 * NONE,
        "pay": np.where((token < TOK)[..., None], pay - 1.0 * NONE, 0.0).reshape(P, 12),
    }
    bands = [band(w) for w in WINDOWS]
    pool = {name: np.concatenate([b[i] for b in bands], 1)
            for i, name in enumerate(("first", "full", "before", "state", "mine"))}
    return early, late, pool, pay.reshape(P, 12).astype(np.int32)


def columns(parts):
    at, out = 0, {}
    for name, a in parts.items():
        out[name] = (at, at + a.shape[1])
        at += a.shape[1]
    return out, at


def build(nc, t):
    early, late, poolc, _ = constants()
    (ce, ne), (cl, nl), (cp, np_) = columns(early), columns(late), columns(poolc)
    ctx = ExitStack()
    with ctx:
        def sb(name, shape, dt=F32):
            return ctx.enter_context(nc.sbuf_tensor(name, shape, dt))

        def sem(name):
            return ctx.enter_context(nc.semaphore(name))

        ring = sb("ring", [P, NSLOT * SLOT + P])
        slot = [ring[:, n * SLOT:(n + 1) * SLOT] for n in range(NSLOT)]
        tok = slot[6].rearrange("p (b c n) -> p b c n", b=PB, c=4)
        qT = slot[7][:, 0:1024].rearrange("p (c n) -> p c n", c=CC)
        kT = slot[7][:, 1024:2048].rearrange("p (c n) -> p c n", c=CC)
        attT = slot[7][:, 2048:2048 + CC * TOK].rearrange("p (c n) -> p c n", c=CC)
        end8 = ring[:, 8 * SLOT:]
        h = end8[:, 0:3 * D].rearrange("p (b n) -> p b n", b=3)
        lfp = end8[:, 3 * D:4 * D]
        lfT = end8[:, 3 * D:3 * D + 512]
        lfC = end8[:, 3 * D + 512:4 * D]
        gates = end8[:, 0:NT * TOK].rearrange("p (n t) -> p n t", n=NT)
        yload = ring[:, 6 * SLOT:9 * SLOT].rearrange("p (b c n) -> p b c n", b=6, c=2)[:, 0:3]

        x = sb("x", [P, 3, D])
        hT = sb("hT", [P, DK, TPAD])
        cea = sb("cea", [P, ne])
        cla = sb("cla", [P, nl])
        E = {n: cea[:, a:b] for n, (a, b) in ce.items()}
        L = {n: cla[:, a:b] for n, (a, b) in cl.items()}
        ident = E["ident"]
        nmix = sb("nmix", [P, DK])
        nffn = sb("nffn", [P, DK])
        pay = sb("pay", [P, 12], I32)
        wf = sb("wf", [P, DK, HEADS])
        wre = sb("wre", [P, GROUPS, DK * PER_GROUP])
        wrg = sb("wrg", [P, DK * GROUPS])
        wr = sb("wr", [P, DK, EXPERTS + GROUPS])
        br = sb("br", [EXPERTS + GROUPS, 1])
        bf = sb("bf", [HEADS, 1])
        pscale = sb("pscale", [P, CC])
        ptab = sb("ptab", [1, NS * PAGES], I32)
        pidx = sb("pidx", [NS * PAGES, 1], I32)
        part = sb("part", [P, DC])
        stat = sb("stat", [P, 32])
        hmax, hsum, hinv = stat[:, 0:2], stat[:, 2:4], stat[:, 4:6]
        nmax, rden, dsc = stat[0:NS, 6:7], stat[0:NS, 7:8], stat[:, 8:16]
        rowsq = sb("rowsq", [P, 3, 1])
        root = sb("root", [P, 3, 1])
        rowt = sb("rowt", [P, 3, 1])

        NFRONT = 7850
        front = sb("front", [P, NFRONT])
        at = [0]

        def carve(n, base=None):
            if base is not None:
                at[0] = base
            at[0] += n
            assert at[0] <= NFRONT, at[0]
            return front[:, at[0] - n:at[0]]

        samp = carve(4 * DC, 0).rearrange("p (c n) -> p c n", c=4)
        qb = carve(DC)
        biasd = carve(DC)
        pooledT = carve(2 * TOK).rearrange("p (i n) -> p i n", i=2)
        mixedT = carve(CC * TOK).rearrange("p (c n) -> p c n", c=CC)
        probs_all = carve(9 * P)
        probs = probs_all[:, 0:6 * P].rearrange("p (i n) -> p i n", i=2)
        probsT = probs_all[:, 6 * P:]
        cpa = end8[:, 0:np_]
        state = end8[:, np_:np_ + DC]
        wpool = end8[:, np_ + DC:np_ + DC + CC * P].rearrange("p (g n) -> p g n", g=CC)
        C = {n: cpa[:, a:b].rearrange("p (g n) -> p g n", g=CC) for n, (a, b) in cp.items()}
        lfd = carve(DC)
        f_ln = lfd[0:HEADS, 0:TOK]
        lf8 = carve(TOK)[0:HEADS]
        cneg = carve(SEQ)[0:HEADS]
        f_z, f_e, f_w, f_min = (probs_all[0:HEADS, i * TOK:(i + 1) * TOK] for i in range(4))
        cq = carve(PB * HEADS).rearrange("p (b n) -> p b n", b=PB)
        lft = carve(3 * HEADS).rearrange("p (b n) -> p b n", b=3)
        snew = carve(NS * HEADS).rearrange("p (b n) -> p b n", b=NS)
        sc = carve(9 * HEADS).rearrange("p (j n) -> p j n", j=9)
        pex = carve(9 * 32).rearrange("p (j n) -> p j n", j=9)
        m1 = carve(HEADS)
        psm = carve(HEADS)
        dg = carve(HEADS)[0:HEADS]
        mk = carve(DC)
        sqout = mixedT.rearrange("p c n -> p (c n)")[:, 0:D]

        xg = carve(512, 0).rearrange("p (i n) -> p i n", i=2)
        xgT = carve(256).rearrange("p (c g s) -> p c g s", c=2, g=4)
        gu = carve(256)
        sg = carve(P).rearrange("p (c g s) -> p c g s", c=2, g=2)
        hE = carve(P).rearrange("p (c g s) -> p c g s", c=2, g=2)
        ysb = carve(512).rearrange("p (i n) -> p i n", i=2)
        normf = carve(D)
        lgT = carve(3 * P)
        lg = carve(3 * 36).rearrange("p (b n) -> p b n", b=3)
        ra = carve(3 * 32).rearrange("p (b n) -> p b n", b=3)
        rb = carve(3 * 32).rearrange("p (b n) -> p b n", b=3)
        em = carve(3 * 32).rearrange("p (b n) -> p b n", b=3)
        e1 = carve(3 * 32).rearrange("p (b n) -> p b n", b=3)
        e2 = carve(3 * 32).rearrange("p (b n) -> p b n", b=3)
        rr = carve(3 * 32).rearrange("p (b n) -> p b n", b=3)
        cs = carve(256)
        over = carve(256)
        ones8 = carve(256)
        sqend = carve(D)
        r_gm, r_m1, r_m2, r_top, r_gs, r_ts, tex = (carve(3).unsqueeze(2) for _ in range(7))
        r_oh, r_t4, gex = (carve(3 * GROUPS).rearrange("p (b n) -> p b n", b=3) for _ in range(3))
        slotpos = carve(6).rearrange("p (b c) -> p b c", b=3)
        rank = carve(6).rearrange("p (b c) -> p b c", b=3)
        selE = carve(3 * 2 * 2 * EXPERTS).rearrange("p (b c i e) -> p b c i e", b=3, c=2, i=2)
        selS = carve(3 * 2 * CAP).rearrange("p (b c s) -> p b c s", b=3, c=2)
        lst = carve(1)

        wts = sb("wts", [P, 2, 3])
        posI = sb("posI", [P, 3, 2], I32)
        gidx = sb("gidx", [P, 2, EXPERTS], I32)
        otab = sb("otab", [P, 2], I32)
        oidx = sb("oidx", [P, 2], I32)
        zeroI = sb("zeroI", [P, 1], I32)
        icolg = sb("icolg", [P, 2], I32)
        icoly = sb("icoly", [P, 2], I32)
        blkI = sb("blkI", [1, 1 + 2 * MAXOVER], I32)
        none = sb("none", [P, RANKS * EXPERTS * 2 // P], I32)

        bank = [ctx.enter_context(nc.psum_tensor(f"bank{i}", [P, 512], F32)) for i in range(8)]
        BIG0, BIG1, PART, SUM, QB, CHAIN, SCORES, TR = range(8)
        filled = [sem(f"bank{i}_filled") for i in range(8)]
        taken = [sem(f"bank{i}_taken") for i in range(8)]

        hs = nc.dram_tensor("h_scratch", [TOK * 4, 256], F32).ap()
        ys = nc.dram_tensor("y_scratch", [TOK * 2 * 4, 256], F32).ap()
        table = nc.dram_tensor("slot_table", [RANKS * EXPERTS, 2], I32).ap()

        PLAN = [("proj", C_Q), ("proj", C_K), ("forget", 0), ("proj", C_V), ("forgetT", 0), ("pages", 0),
                ("dq", 0), ("keys0", 0), ("keys1", 0)] + [("qk", i) for i in range(4)] + [
                ("bias", 0), ("proj", C_U), ("keys2", 0), ("keys3", 0)]
        PLAN += [("dmax", 0), ("pool", 0), ("dshift", 0)] + [("pool", g) for g in range(1, CC + 1)]
        for b in range(1, NS + 1):
            now = b < NS
            PLAN += [("hnorm", b - 2)] * (b > 1) + [("dq", b), ("keys0", b)] * now
            PLAN += [("gate", 2 * b - 2)] + [("keys1", b)] * now + [("head", b - 1), ("dpv", b - 1)]
            PLAN += [("keys2", b)] * now + [("gate", 2 * b - 1)] + [("keys3", b)] * now
            PLAN += [("dsum", b - 1)] + [("up", b - 1), ("dmax", b)] * now + [("pv", b - 2)] * (b > 1) + [("datt", b - 1)] + [("dshift", b)] * now
        PLAN += [("hnorm", HEADS - 1), ("head", HEADS), ("up", DK - 1), ("pv", HEADS - 1)]
        PLAN += [("merge", n) for n in range(DK)] + [("out", 0), ("norm", 0), ("route", 0)]

        uses = {("w", c): (("proj", c), ("proj", c)) for c in range(4)}
        uses.update({("g", n): (("gate", GPS * n), ("gate", GPS * n + GPS - 1)) for n in range(4)})
        for b in range(NS):
            uses["K", b] = ("keys0", b), ("keys3", b)
            uses["V", b] = ("dpv", b), ("dpv", b)
        uses["up", 0] = ("up", 0), ("up", DK - 1)
        uses["up", 1] = ("merge", 0), ("merge", DK - 1)
        uses["out", 0] = uses["out", 1] = ("out", 0), ("out", 0)
        STREAM = sorted(uses, key=lambda item: PLAN.index(uses[item][0]))
        last_step, where, before = [-1] * FRONT, {}, {}
        for item in STREAM:
            q = last_step.index(min(last_step))
            before[item] = [i for i in where if where[i] == q][-1:]
            where[item], last_step[q] = q, PLAN.index(uses[item][1])
        loaded, slot_count = {}, [0] * NSLOT
        for item in STREAM:
            slot_count[where[item]] += 16 * (PAGES if item[0] in "KV" else 1)
            loaded[item] = slot_count[where[item]]
        SLOT_BASE = list(slot_count)
        last_step += [PLAN.index(("pv", HEADS - 1)), PLAN.index(("merge", DK - 1)), len(PLAN)]
        FREED = sorted(range(NSLOT), key=lambda q: last_step[q])

        turn, fills, big = {}, [0] * 8, [0]

        def assign(b, *label):
            if b is None:
                b = (BIG0, BIG1)[big[0] % 2]
                big[0] += 1
            turn[label] = (b, fills[b])
            fills[b] += 1

        TPOSE = [(QB, 2, 0), (BIG0, 0, 0), (BIG1, 0, 1), (SCORES, 1, 0), (TR, 1, 1)]
        for i, (b, _, _) in enumerate(TPOSE):
            assign(b, "hT", 0, i)
        for step, a in PLAN:
            if step == "proj":
                assign(PART, "part", a), assign(SUM, "sum", a), assign(None, "proj", a, 0), assign(None, "proj", a, 1)
            elif step == "forget":
                assign(CHAIN, "forget")
            elif step == "forgetT":
                assign(CHAIN, "forgetT")
            elif step == "pages":
                assign(SCORES, "pagesT")
            elif step == "bias":
                assign(SCORES, "bias")
            elif step == "qk":
                assign((TR, SCORES)[a % 2], "qk", a)
            elif step == "dq":
                assign(QB, "dq", a)
            elif step in ("dmax", "dshift", "datt"):
                assign(CHAIN, step, a)
            elif step == "dpv":
                assign(PART, "dpv", a), assign(CHAIN, "den", a)
            elif step == "dsum":
                assign(SUM, "dsum", a)
            elif step == "pool":
                if a < CC:
                    assign(None, "pool", a)
                if a:
                    assign(None, "mix", a - 1)
            elif step in ("gate", "up", "merge"):
                assign(None, step, a)
            elif step == "head":
                if a < HEADS:
                    assign(SCORES, "scores", a)
                if a:
                    assign(TR, "pT", a - 1)
            elif step == "pv":
                assign(TR, "pv", a)
            elif step == "out":
                for half in range(2):
                    assign((PART, QB)[half], "opart", half), assign(SUM, "osum", half)
                for i in range(4):
                    assign((BIG0, BIG1, SCORES, TR)[i], "out", i)
            elif step == "norm":
                for i, (b, _, _) in enumerate(TPOSE):
                    assign(b, "hT", 1, i)
            elif step == "route":
                assign(PART, "logits"), assign(SUM, "logitsT"), assign(BIG0, "ranks"), assign(BIG1, "slots"), assign(CHAIN, "blocks")

        s_slot = [sem(f"slot{i}_loaded") for i in range(NSLOT)]
        in_xs, in_xp, in_ce, in_cl, in_nm, in_wf, in_ptab, in_pidx, in_pool, in_route, in_nf, in_lfp = (
            sem(n) for n in ("x_sample_in", "x_prompt_in", "early_consts_in", "late_consts_in", "norm_mix_in", "forget_weights_in",
                             "page_table_in", "page_index_in", "pool_weights_in", "router_in", "norm_final_in", "page_forgets_in"))
        out_tok, out_pool, out_y = sem("prompt_rows_written"), sem("outputs_written_by_pool"), sem("y_written")
        l_dve = sem("dve_link")
        s_sq, l_act, s_h, s_pad = sem("rough_roots_ready"), sem("act_link"), sem("rows_normalised"), sem("pads_set")
        s_fz, s_fexp, s_fw, s_fln, s_lf, s_lfd = (sem(n) for n in (
            "forget_logits_ready", "forget_exp", "forget_exp_plus_one", "forget_ln", "log_forget_ready", "page_forgets_summed"))
        s_kused, s_m1, s_dg, s_pex, s_psm, s_rden = (sem(n) for n in (
            "K_slots_used", "page_max_ready", "max_diagonal_ready", "decode_probs_ready", "prob_sums_ready", "inverse_sums_ready"))
        s_kprod = sem("key_products_ready")
        s_rmax, s_exp, s_probs, s_merge = sem("row_max_ready"), sem("prompt_exp_ready"), sem("probs_ready"), sem("branches_merged")
        s_hs, s_gsh, s_gex, s_tsh, s_tex = (sem(n) for n in (
            "h2_written", "group_logits_shifted", "group_exp_ready", "top_logits_shifted", "top_exp_ready"))
        s_rr, s_sel, s_pos, s_scat, s_idx, s_none, s_clear = (sem(n) for n in (
            "routed_ready", "slot_factors_ready", "positions_ready", "table_written", "indices_ready", "sentinel_made", "table_cleared"))
        s_wr = sem("router_ready")
        s_otab, s_oidx = sem("later_table_read"), sem("later_indices_ready")
        s_lst, s_icg, s_icy = sem("blocks_listed"), sem("gather_index_ready"), sem("scatter_index_ready")
        s_xt, s_xgT, s_gu, s_gusb, s_guT, s_sg, s_hE, s_dn, s_ysb = (sem(n) for n in (
            "tokens_transposed", "tokensT_ready", "gate_up_in_psum", "gate_up_copied", "gate_up_transposed",
            "silu_ready", "hidden_ready", "down_in_psum", "expert_rows_ready"))
        s_xg, s_yst = ([sem(f"{n}{i}") for i in range(2)] for n in ("tokens_gathered", "expert_rows_scattered"))
        s_yl = [sem(f"expert_rows_loaded{i}") for i in range(3)]
        s_zero, s_x3, s_fin = sem("gather_buffer_zeroed"), sem("residual_added"), sem("final_rows_ready")

        w_in = t["w_in"][0]
        cache = {"K": t["cache_k"][0].rearrange("g r h d -> g r (h d)"), "V": t["cache_v"][0].rearrange("g r h d -> g r (h d)")}
        y_rows = ys.rearrange("(t c q) n -> t c (q n)", c=2, q=4)
        h_rows = hs.rearrange("(t q) n -> t (q n)", q=4)
        ident8 = ident[0:NS, 0:NS]
        ones = L["ones"]
        BLOCKS = ((2, NS), (0, P), (1, P))

        def count_full(*label):
            b, n = turn[label]
            return filled[b], n + 1

        def count_taken(*label):
            b, n = turn[label]
            return taken[b], n + 1

        last_use = {("w", c): ("proj", c, 1) for c in range(4)}
        last_use.update({("g", n): ("gate", GPS * n + GPS - 1) for n in range(4)})
        last_use.update({("V", b): ("dpv", b) for b in range(NS)})
        last_use.update({("up", 0): ("up", DK - 1), ("up", 1): ("merge", DK - 1), ("out", 0): ("out", 2 * PB - 1), ("out", 1): ("out", 2 * PB - 1)})

        def count_used(item):
            return (s_kused, 4 * item[1] + 4) if item[0] == "K" else count_full(*last_use[item])

        def wait_loaded(eng, *item):
            eng.wait_ge(s_slot[where[item]], loaded[item])
            return slot[where[item]]

        def load_matrix(eng, e, m, q):
            src = t[("w_gate", "w_up", "w_down")[m]][0, bass.ds(e, 1)]
            if m < 2:
                eng.dma_start(slot[q], src.rearrange("e (p k) f -> p (e k f)", p=P)).then_inc(s_slot[q], 16)
            else:
                eng.dma_start(slot[q].rearrange("p (j n) -> p j n", j=FC), src.rearrange("e (j p) n -> p (e j) n", p=P)).then_inc(s_slot[q], 16)

        AFTER = [SLOT_BASE[m] + 16 * len(range(0, EXPERTS, 3)) for m in range(3)]
        by_block = table.rearrange("(j s e) c -> j s e c", s=CAP, e=EXPERTS)

        def later_blocks(eng, step, before=lambda: None):
            eng.wait_ge(*count_taken("blocks"))
            count = eng.value_load(blkI[0:1, 0:1], min_val=0, max_val=MAXOVER)
            with eng.If(count > 0):
                before()
                with eng.Fori(0, count) as r:
                    step(r)
            return count

        block = ctx.enter_context(nc.Block())

        @block.sync
        def _(sp):
            sp.dma_start(x[0:NS, 2, :], t["x_sample"].rearrange("b s d -> (b s) d")).then_inc(in_xs, 16)
            sp.dma_start(cea[:], t["c_early"]).then_inc(in_ce, 16)
            sp.dma_start(x[:, 0:PB, :], t["x_prompt"][0].rearrange("(b p) d -> p b d", p=P)).then_inc(in_xp, 16)
            for item in STREAM:
                for last in before[item]:
                    sp.wait_ge(*count_used(last))
                kind, a = item
                dst, done = slot[where[item]], s_slot[where[item]]
                if kind in "wg":
                    first = a * DC if kind == "w" else W_GATE + a * DC
                    sp.dma_start(dst.rearrange("p (k n) -> p k n", k=DK),
                                 w_in[:, first:first + DC].rearrange("(p k) n -> p k n", p=P)).then_inc(done, 16)
                elif kind in "KV":
                    if item == ("K", 0):
                        sp.wait_ge(in_ptab, 16)
                    for j in range(PAGES):
                        page = sp.value_load(ptab[0:1, a * PAGES + j:a * PAGES + j + 1], min_val=0, max_val=NPHYS - 1)
                        sp.dma_start(dst[:, j * DC:(j + 1) * DC],
                                     cache[kind][bass.ds(page, 1)].rearrange("g r n -> (g r) n")).then_inc(done, 16)
                else:
                    src = (t["w_up_pool"][0] if a == 0 else t["w_up_att"][0]) if kind == "up" else t["w_out"][0, a * DC:(a + 1) * DC]
                    sp.dma_start(dst.rearrange("p (k n) -> p k n", k=CC), src.rearrange("(k p) n -> p k n", p=P)).then_inc(done, 16)
            for q in FREED:
                if q < FRONT:
                    sp.wait_ge(*count_used([i for i in STREAM if where[i] == q][-1]))
                elif q == 6:
                    sp.wait_ge(*count_full("pv", HEADS - 1))
                    sp.wait_ge(*count_full("pool", CC - 1))
                    sp.wait_ge(out_tok, 16 * 3)
                elif q == 7:
                    sp.wait_ge(*count_full("merge", DK - 1))
                else:
                    sp.wait_ge(s_hs, 16 * 2)
                    for i in range(len(TPOSE)):
                        sp.wait_ge(*count_full("hT", 1, i))
                load_matrix(sp, q // 3, q % 3, q)
            with sp.Fori(0, (EXPERTS - 5) // 3) as i:
                for r in range(3):
                    sp.wait_ge(s_gu, 3 * i + r + 1)
                    load_matrix(sp, 3 * i + (3 + r), 0, 3 * r)
                    load_matrix(sp, 3 * i + (3 + r), 1, 3 * r + 1)
                    sp.wait_ge(s_dn, 3 * i + r + 1)
                    load_matrix(sp, 3 * i + (3 + r), 2, 3 * r + 2)
            for e in range(EXPERTS - 2, EXPERTS):
                sp.wait_ge(s_gu, e - 2)
                load_matrix(sp, e, 0, 3 * (e % 3))
                load_matrix(sp, e, 1, 3 * (e % 3) + 1)
                sp.wait_ge(s_dn, e - 2)
                load_matrix(sp, e, 2, 3 * (e % 3) + 2)

            def later_block(r):
                sp.wait_ge(s_dn, r + EXPERTS)
                e = sp.value_load(blkI[0:1, bass.ds(r + 1, 1)], min_val=0, max_val=EXPERTS - 1)
                for mat in range(3):
                    load_matrix(sp, e, mat, mat)
                j = sp.value_load(blkI[0:1, bass.ds(r + (1 + MAXOVER), 1)], min_val=0, max_val=7)
                for q in range(4):
                    sp.dma_start(otab[CAP * q:CAP * (q + 1)], by_block[bass.ds(j + 1, 1), :, bass.ds(e, 1)].rearrange("j s e c -> (j s) (e c)")).then_inc(s_otab, 16)
            n_later = later_blocks(sp, later_block, lambda: sp.wait_ge(s_scat, 16 * 6))
            sp.wait_ge(s_yst[0], 16 * n_later + 8 * EXPERTS)
            sp.wait_ge(s_yst[1], 8 * EXPERTS)
            sp.dma_start(yload[0:NS, 2], y_rows[SEQ:TOK]).then_inc(s_yl[0], 16)
            sp.dma_start(yload[:, 0], y_rows[0:P]).then_inc(s_yl[1], 16)
            sp.dma_start(yload[:, 1], y_rows[P:2 * P]).then_inc(s_yl[2], 16)
            y_out = t["y_prompt"][0].rearrange("(b p) d -> p b d", p=P)
            sp.wait_ge(s_fin, 1)
            sp.dma_start(t["y_sample"].rearrange("b s d -> (b s) d"), x[0:NS, 2, :]).then_inc(out_y, 16)
            for b in range(PB):
                sp.wait_ge(s_fin, b + 2)
                sp.dma_start(y_out[:, b], x[:, b, :]).then_inc(out_y, 16)
            sp.wait_ge(out_y, 16 * 3)
            sp.wait_ge(out_tok, 16 * 3)
            sp.wait_ge(out_pool, 16 * 6)

        @block.gpsimd
        def _(pool):
            g = nc.gpsimd
            g.memset(none[:], NONE).then_inc(s_none, 1)
            pool.wait_ge(s_none, 1)
            g.dma_start(table.rearrange("(p n) c -> p (n c)", p=P), none[:]).then_inc(s_clear, 16)
            g.dma_start(t["new_pool_sample"][0, :, 0:PLEN - 1, :], t["state_pool"][0, :, 1:PLEN, :]).then_inc(out_pool, 16)
            pool.wait_ge(in_pidx, 16)
            g.indirect_dma_start(lfp[0:NS * PAGES, :], None, t["cache_logf"][0].rearrange("g r h -> g (r h)"),
                                 bass.IndirectOffsetOnAxis(pidx[:, 0:1], 0), bounds_check=NPHYS - 1).then_inc(in_lfp, 16)
            pool.wait_ge(in_route, 16 * 6)
            g.tensor_copy(wr[:, :, 0:EXPERTS].rearrange("p k (g e) -> p k g e", g=GROUPS), wre[:].rearrange("p g (k e) -> p k g e", k=DK)).then_inc(s_wr, 1)
            g.tensor_copy(wr[:, :, EXPERTS:], wrg[:].rearrange("p (k g) -> p k g", k=DK)).then_inc(s_wr, 1)
            for step, a in PLAN:
                if step == "forgetT":
                    pool.wait_ge(*count_taken("forgetT"))
                    g.dma_start(t["new_logf_prompt"][0, 0].rearrange("(b p) n -> p b n", p=P), lft[:, 0:2]).then_inc(out_pool, 16)
                    g.dma_start(t["new_logf_sample"][0, :, 0], lft[0:NS, 2]).then_inc(out_pool, 16)
                elif step == "proj" and a != C_Q:
                    for b in range(PB):
                        pool.wait_ge(*count_taken("proj", a, b))
                    pool.wait_ge(*count_taken("sum", a))
                    if a == C_U:
                        g.dma_start(t["new_pool_prompt"][0, 0], tok[P - PLEN:P, 1, C_U, :]).then_inc(out_tok, 16)
                        g.dma_start(t["new_pool_sample"][0, :, PLEN - 1, :], samp[0:NS, C_U, :]).then_inc(out_pool, 16)
                    else:
                        k = "k" if a == C_K else "v"
                        g.dma_start(t[f"new_{k}_prompt"][0, 0].rearrange("(b p) h d -> p b (h d)", p=P), tok[:, :, a, :]).then_inc(out_tok, 16)
                        g.dma_start(t[f"new_{k}_sample"][0, :, 0].rearrange("b h d -> b (h d)"), samp[0:NS, a, :]).then_inc(out_pool, 16)
            pool.wait_ge(s_zero, 1)
            pool.wait_ge(s_hs, 16 * 2)
            pool.wait_ge(s_idx, 1)
            nought = pool.alloc_register("nought")
            pool.reg_mov(nought, 0)
            g.memset(zeroI[:], 0).then_inc(s_none, 1)
            pool.wait_ge(s_none, 2)
            h_last, y_last = pool.alloc_register("last_h_row"), pool.alloc_register("last_y_row")

            def gather(n, p, rows):
                g.tensor_tensor(icolg[:, p:p + 1], rows, zeroI[:], ALU.add).then_inc(s_icg, 1)
                pool.wait_ge(s_icg, n + 1)
                pool.reg_add(h_last, nought, TOK * 4 - 1)
                g.indirect_dma_start(xg[:, p], None, hs, bass.IndirectOffsetOnAxis(icolg[:, p:p + 1], 0),
                                     bounds_check=h_last, oob_is_err=False).then_inc(s_xg[p], 16)

            def scatter(n, p, rows):
                pool.wait_ge(s_ysb, n + 1)
                g.tensor_tensor(icoly[:, p:p + 1], rows, zeroI[:], ALU.add).then_inc(s_icy, 1)
                pool.wait_ge(s_icy, n + 1)
                pool.reg_add(y_last, nought, TOK * 8 - 1)
                g.indirect_dma_start(ys, bass.IndirectOffsetOnAxis(icoly[:, p:p + 1], 0), ysb[:, p], None,
                                     bounds_check=y_last, oob_is_err=False).then_inc(s_yst[p], 16)

            for p in range(2):
                gather(p, p, gidx[:, 0, p:p + 1])
            with pool.Fori(0, EXPERTS // 2 - 1) as i:
                for p in range(2):
                    pool.wait_ge(s_xt, 2 * i + p + 1)
                    gather(2 * i + (p + 2), p, gidx[:, 0, bass.ds(2 * i + (p + 2), 1)])
                    scatter(2 * i + p, p, gidx[:, 1, bass.ds(2 * i + p, 1)])
            for e in range(EXPERTS - 2, EXPERTS):
                scatter(e, e % 2, gidx[:, 1, e:e + 1])

            def later_block(r):
                pool.wait_ge(s_oidx, r + 1)
                gather(r + EXPERTS, 0, oidx[:, 0:1])
                scatter(r + EXPERTS, 0, oidx[:, 1:2])

            def scatter_table():
                pool.wait_ge(s_clear, 16)
                pool.wait_ge(s_pos, 1)
                for b in range(3):
                    n = NS if b == 2 else P
                    for c in range(2):
                        g.indirect_dma_start(table, bass.IndirectOffsetOnAxis(posI[0:n, b, c:c + 1], 0),
                                             pay[0:n, 4 * b + 2 * c:4 * b + 2 * c + 2], None, bounds_check=RANKS * EXPERTS - 1).then_inc(s_scat, 16)
            later_blocks(pool, later_block, scatter_table)

        @block.scalar
        def _(act):
            s = nc.scalar
            act.dma_start(nmix[:], t["norm_mix"][0].rearrange("(p k) -> p k", p=P)).then_inc(in_nm, 16)
            act.dma_start(pidx[:], t["page_table"].rearrange("b (j o) -> (b j) o", o=1)).then_inc(in_pidx, 16)
            act.dma_start(ptab[:], t["page_table"].rearrange("(o b) j -> o (b j)", o=1)).then_inc(in_ptab, 16)
            act.dma_start(wf[:], w_in[:, W_FORGET:W_FORGET + HEADS].rearrange("(p k) n -> p k n", p=P)).then_inc(in_wf, 16)
            act.dma_start(bf[:], t["b_forget"].rearrange("o n -> n o")).then_inc(in_wf, 16)

            def full(*label):
                act.wait_ge(*count_full(*label))
                return bank[turn[label][0]]

            links = [0]

            def link(ins):
                links[0] += 1
                ins.then_inc(l_act, 1)
                act.wait_ge(l_act, links[0])

            squared = [0]

            def mean_square(b, n, out):
                if squared[0]:
                    act.wait_ge(s_sq, squared[0])
                squared[0] += 1
                s.activation(out[0:n, :], x[0:n, b, :], ACT.Square, scale=D ** -0.5, accum_out=rowsq[0:n, b]).then_inc(s_sq, 1)

            act.wait_ge(s_pad, 4)
            for b, n in BLOCKS:
                act.wait_ge(*((in_xs, 16) if b == 2 else (in_xp, 16)))
                mean_square(b, n, sqout)
            act.dma_start(cla[:], t["c_late"]).then_inc(in_cl, 16)
            act.dma_start(nffn[:], t["norm_ffn"][0].rearrange("(p k) -> p k", p=P)).then_inc(in_route, 16)
            act.dma_start(wre[:], t["w_router_expert"][0].rearrange("g (p k) e -> p g (k e)", p=P)).then_inc(in_route, 16)
            act.dma_start(wrg[:], t["w_router_group"][0].rearrange("(p k) g -> p (k g)", p=P)).then_inc(in_route, 16)
            act.dma_start(br[0:EXPERTS], t["b_router_expert"][0].rearrange("g (e o) -> (g e) o", o=1)).then_inc(in_route, 16)
            act.dma_start(br[EXPERTS:EXPERTS + GROUPS], t["b_router_group"].rearrange("o n -> n o")).then_inc(in_route, 16)
            act.dma_start(pay[:], t["c_pay"]).then_inc(in_route, 16)
            for i in range(len(TPOSE)):
                act.wait_ge(*count_full("hT", 0, i))
            act.dma_start(cpa[:], t["c_pool"]).then_inc(in_pool, 16)
            act.dma_start(state[0:NS * PLEN, :], t["state_pool"][0].rearrange("b j n -> (b j) n")).then_inc(in_pool, 16)
            act.dma_start(wpool[:], t["w_pool"][0].rearrange("g p n -> p g n")).then_inc(in_pool, 16)
            act.dma_start(pscale[:], t["pool_scale"][0].rearrange("(g p) -> p g", p=P), allow_slow_non_contiguous=True).then_inc(in_pool, 16)

            for step, a in PLAN:
                if step == "proj":
                    src = full("part", a)
                    if turn["sum", a][1]:
                        act.wait_ge(filled[SUM], turn["sum", a][1])
                    s.copy(part[:], src[:]).then_inc(taken[PART], 1)
                    for b in range(PB):
                        src = full("proj", a, b)
                        s.copy(tok[:, b, a, :], src[:]).then_inc(taken[turn["proj", a, b][0]], 1)
                elif step == "forget":
                    act.wait_ge(s_fz, 1)
                    link(s.activation(f_e, f_z, ACT.Abs))
                    s.activation(f_e, f_e, ACT.Exp, scale=-1.0).then_inc(s_fexp, 1)
                    act.wait_ge(s_fw, 1)
                    s.activation(f_ln, f_w, ACT.Ln).then_inc(s_fln, 1)
                elif step == "pages":
                    s.copy(lfT, full("pagesT")[:]).then_inc(taken[SCORES], 1)
                elif step == "bias":
                    s.copy(biasd, full("bias")[:]).then_inc(taken[SCORES], 1)
                elif step == "qk":
                    out = (qT, kT)[a // 2][:, :, (a % 2) * P:(a % 2 + 1) * P]
                    src = full("qk", a)[:].rearrange("p (c n) -> p c n", c=CC)
                    s.activation(out, src, ACT.Copy, scale=QSCALE if a < 2 else 1.0).then_inc(taken[turn["qk", a][0]], 1)
                elif step == "dq":
                    src = full("dq", a)
                    if a:
                        act.wait_ge(s_kprod, 4 * a)
                    s.activation(qb, src[:], ACT.Copy, scale=QSCALE).then_inc(taken[QB], 1)
                elif step == "dshift":
                    act.wait_ge(*count_taken("dshift", a))
                    if a:
                        act.wait_ge(*count_full("den", a - 1))
                    else:
                        act.wait_ge(s_pad, 3)
                    s.activation(pex[:, :, 0:HEADS], sc, ACT.Exp).then_inc(s_pex, 1)
                elif step == "dpv":
                    src = full("dpv", a)
                    act.wait_ge(filled[SUM], turn["dsum", a][1])
                    s.copy(part[:], src[:]).then_inc(taken[PART], 1)
                elif step == "pool":
                    if a < CC:
                        src = full("pool", a)
                        if a >= 2:
                            act.wait_ge(*count_full("mix", a - 2))
                        s.copy(pooledT[:, a % 2], src[:, 0:TOK]).then_inc(taken[turn["pool", a][0]], 1)
                    if a:
                        src = full("mix", a - 1)
                        if a == 1:
                            act.wait_ge(in_pool, 16 * 4)
                        s.activation(mixedT[:, a - 1], src[:, 0:TOK], ACT.Copy, scale=pscale[:, a - 1:a]).then_inc(taken[turn["mix", a - 1][0]], 1)
                elif step == "gate":
                    src = full("gate", a)
                    s.activation(gates[:, a], src[:, 0:TOK], ACT.Tanh, scale=0.5).then_inc(taken[turn["gate", a][0]], 1)
                elif step == "head":
                    if a:
                        src = full("pT", a - 1)
                        if a >= 2:
                            act.wait_ge(*count_full("pv", a - 2))
                        s.copy(probsT, src[:, 0:3 * P]).then_inc(taken[TR], 1)
                    if a < HEADS:
                        act.wait_ge(s_rmax, a + 1)
                        pr = probs[:, a % 2]
                        s.activation(pr[:, 0:P], pr[:, 0:P], ACT.Exp, bias=hmax[:, 0:1], accum_out=hsum[:, 0:1]).then_inc(s_exp, 1)
                        s.activation(pr[:, P:3 * P], pr[:, P:3 * P], ACT.Exp, bias=hmax[:, 1:2], accum_out=hsum[:, 1:2]).then_inc(s_exp, 1)
                elif step == "out":
                    for half in range(2):
                        src = full("opart", half)
                        act.wait_ge(filled[SUM], turn["osum", half][1])
                        s.copy(part[:], src[:]).then_inc(taken[turn["opart", half][0]], 1)
                elif step == "norm":
                    act.wait_ge(s_pad, 5)
                    for i, (b, n) in enumerate(BLOCKS):
                        if b == 2:
                            act.wait_ge(*count_taken("osum", 1))
                            act.wait_ge(*count_full("up", DK - 1))
                        else:
                            act.wait_ge(*count_taken("out", 2 * b))
                            act.wait_ge(*count_taken("out", 2 * b + 1))
                        mean_square(b, n, sqout)
                    act.wait_ge(s_h, 4)
                    act.dma_start(h_rows[SEQ:TOK], h[0:NS, 2]).then_inc(s_hs, 16)
                    act.wait_ge(s_h, 6)
                    act.dma_start(h_rows[0:SEQ].rearrange("(b p) n -> p b n", p=P), h[:, 0:PB]).then_inc(s_hs, 16)
                elif step == "route":
                    act.wait_ge(out_pool, 16 * 6)
                    act.dma_start(normf[:], t["norm_final"].partition_broadcast(P)).then_inc(in_nf, 16)
                    act.wait_ge(s_gsh, 1)
                    s.activation(gex, gex, ACT.Exp).then_inc(s_gex, 1)
                    act.wait_ge(s_tsh, 1)
                    s.activation(tex, tex, ACT.Exp).then_inc(s_tex, 1)

            def hidden(n):
                act.wait_ge(s_guT, n + 1)
                s.activation(sg, bank[QB][:, 0:256].rearrange("p (c g s) -> p c g s", c=2, g=4)[:, :, 0:2], ACT.Silu).then_inc(s_sg, 1)

            with act.Fori(0, EXPERTS) as e:
                hidden(e)
            later_blocks(act, lambda r: hidden(r + EXPERTS))
            act.wait_ge(s_pad, 6)
            for i, (b, n) in enumerate(BLOCKS):
                act.wait_ge(s_x3, i + 1)
                mean_square(b, n, sqend)

        @block.vector
        def _(dve):
            v = nc.vector
            links = [0]

            def link(ins):
                links[0] += 1
                ins.then_inc(l_dve, 1)
                dve.wait_ge(l_dve, links[0])

            def full(*label):
                dve.wait_ge(*count_full(*label))
                return bank[turn[label][0]]

            v.memset(hT[:, :, TOK:TPAD], 0.0).then_inc(s_pad, 1)
            v.memset(pex, 0.0).then_inc(s_pad, 1)
            v.memset(snew, -BIG).then_inc(s_pad, 1)
            v.memset(rowsq[:], 1.0).then_inc(s_pad, 1)

            def roots(blocks, n):
                a, r, t2 = rowsq[0:n, blocks], root[0:n, blocks], rowt[0:n, blocks]
                link(v.tensor_scalar(a, a, EPS, None, ALU.add))
                link(v.tensor_scalar(r.bitcast(I32), a.bitcast(I32), 1, None, ALU.logical_shift_right))
                link(v.tensor_scalar(r.bitcast(I32), r.bitcast(I32), -1.0, float(0x5f3759df), ALU.mult, ALU.add))
                link(v.tensor_scalar(a, a, -0.5, None, ALU.mult))
                for _ in range(3):
                    link(v.tensor_tensor(t2, r, r, ALU.mult))
                    link(v.tensor_tensor(t2, t2, a, ALU.mult))
                    link(v.scalar_tensor_tensor(r, t2, 1.5, r, ALU.add, ALU.mult))

            def normalise(b, n):
                v.tensor_scalar(h[0:n, b].rearrange("t (k p) -> t p k", k=DK), x[0:n, b].rearrange("t (p k) -> t p k", k=DK), root[0:n, b], None,
                                ALU.mult).then_inc(s_h, 1)

            def transposed(which, norm, banks):
                for i in banks:
                    k, b, half = TPOSE[i]
                    src = full("hT", which, i)
                    if b == 2:
                        v.tensor_tensor(hT[:, :, SEQ:TOK], src[:, 0:DK * NS].rearrange("p (k t) -> p k t", k=DK),
                                        norm[:].unsqueeze(2).to_broadcast([P, DK, NS]), ALU.mult).then_inc(taken[k], 1)
                    else:
                        ks = slice(4 * half, 4 * half + 4)
                        v.tensor_tensor(hT[:, ks, b * P:(b + 1) * P], src[:].rearrange("p (k t) -> p k t", k=4),
                                        norm[:, ks].unsqueeze(2).to_broadcast([P, 4, P]), ALU.mult).then_inc(taken[k], 1)

            dve.wait_ge(s_sq, 3)
            roots(slice(0, 3), P)
            v.memset(rowsq[:], 1.0).then_inc(s_pad, 1)
            for b, n in BLOCKS:
                normalise(b, n)
            dve.wait_ge(in_nm, 16)
            transposed(0, nmix, range(5))

            def add_out(i):
                xs = x[:, i // 2, (i % 2) * 512:(i % 2 + 1) * 512]
                v.scalar_tensor_tensor(xs, full("out", i)[:], 0.5, xs, ALU.mult, ALU.add).then_inc(taken[turn["out", i][0]], 1)

            def run_plan():
                for step, a in PLAN:
                    if step == "proj":
                        v.tensor_copy(samp[0:NS, a, :], full("sum", a)[0:NS, :]).then_inc(taken[SUM], 1)
                    elif step == "forget":
                        dve.wait_ge(in_wf, 32)
                        v.tensor_scalar(f_z, full("forget")[0:HEADS, 0:TOK], bf[:, 0:1], None, ALU.add).then_inc(s_fz, 1)
                        dve.wait_ge(s_fz, 1)
                        v.tensor_scalar(f_min, f_z, 0.0, None, ALU.min).then_inc(taken[CHAIN], 1)
                        dve.wait_ge(s_fexp, 1)
                        v.tensor_scalar(f_w, f_e, 1.0, None, ALU.add).then_inc(s_fw, 1)
                        dve.wait_ge(s_fw, 1)
                        link(v.tensor_scalar(f_z, f_w, 1.0, None, ALU.subtract))
                        dve.wait_ge(s_fln, 1)
                        link(v.tensor_tensor(f_ln, f_ln, f_e, ALU.mult))
                        link(v.tensor_scalar(f_w, f_z, 1e-30, None, ALU.max))
                        link(v.reciprocal(f_w, f_w))
                        link(v.tensor_tensor(f_ln, f_ln, f_w, ALU.mult))
                        link(v.tensor_scalar(f_z, f_z, 0.0, None, ALU.is_equal))
                        link(v.tensor_tensor(f_z, f_z, f_e, ALU.mult))
                        link(v.tensor_tensor(f_ln, f_ln, f_z, ALU.add))
                        link(v.tensor_tensor(lf8, f_min, f_ln, ALU.subtract))
                        link(v.memset(f_w, 1.0))
                        link(v.tensor_tensor_scan(f_e[:, 0:SEQ], f_w[:, 0:SEQ], lf8[:, 0:SEQ], 0.0, ALU.mult, ALU.add))
                        v.tensor_scalar(cneg, f_e[:, 0:SEQ], -1.0, None, ALU.mult).then_inc(s_lf, 1)
                    elif step == "forgetT":
                        src = full("forgetT")
                        link(v.tensor_scalar(cq, src[:, 0:16].rearrange("p (b n) -> p b n", b=2), -1.0, None, ALU.mult))
                        link(v.tensor_copy(lft[:, 0:2], src[:, 16:32].rearrange("p (b n) -> p b n", b=2)))
                        v.tensor_copy(lft[0:NS, 2], src[0:NS, 32:40]).then_inc(taken[CHAIN], 1)
                    elif step == "pages":
                        dve.wait_ge(in_cl, 16)
                        dve.wait_ge(*count_taken("sum", C_V))
                        dve.wait_ge(s_pad, 3)
                        link(v.tensor_tensor(mk[0:NS], samp[0:NS, C_Q, :], samp[0:NS, C_K, :], ALU.mult))
                        link(v.tensor_reduce(dsc[0:NS, 0:HEADS], mk[0:NS].rearrange("p (h d) -> p h d", h=HEADS), AX.X, ALU.add))
                        link(v.tensor_scalar(dsc[0:NS, 0:HEADS], dsc[0:NS, 0:HEADS], QSCALE, None, ALU.mult))
                        link(v.tensor_tensor(snew[0:NS], dsc[0:NS, 0:HEADS].unsqueeze(1).to_broadcast([NS, NS, HEADS]),
                                        L["other"][0:NS].unsqueeze(2).to_broadcast([NS, NS, HEADS]), ALU.add))
                        dve.wait_ge(*count_taken("pagesT"))
                        lt = lfT.rearrange("p (m j) -> p m j", j=PAGES)
                        lc = lfC.rearrange("p (m j) -> p m j", j=PAGES)
                        link(v.memset(lc[:, :, PAGES - 1], 0.0))
                        for j in range(PAGES - 2, -1, -1):
                            link(v.tensor_tensor(lc[:, :, j], lc[:, :, j + 1], lt[:, :, j + 1], ALU.add))
                        dve.wait_ge(*count_taken("forgetT"))
                        v.tensor_tensor(lfd.rearrange("p (h b j) -> p h b j", h=HEADS, b=NS)[0:NS],
                                        lft[0:NS, 2].unsqueeze(2).unsqueeze(3).to_broadcast([NS, HEADS, NS, PAGES]),
                                        ident8.unsqueeze(1).unsqueeze(3).to_broadcast([NS, HEADS, NS, PAGES]), ALU.mult).then_inc(s_lfd, 1)
                    elif step[:4] == "keys":
                        part_ = int(step[4:])
                        ks = wait_loaded(dve, "K", a).rearrange("p (j n) -> p j n", j=PAGES)[:, 2 * part_:2 * part_ + 2]
                        dve.wait_ge(*count_taken("dq", a))
                        v.tensor_tensor(ks, ks, qb.unsqueeze(1).to_broadcast([P, 2, DC]), ALU.mult).then_inc(s_kprod, 1)
                        dve.wait_ge(s_kprod, 4 * a + part_ + 1)
                        if a:
                            dve.wait_ge(s_pex, a)
                        v.tensor_reduce(sc[:, 2 * part_:2 * part_ + 2], ks.rearrange("p j (h d) -> p j h d", h=HEADS), AX.X, ALU.add).then_inc(s_kused, 1)
                        if part_ == PAGES // 2 - 1:
                            dve.wait_ge(s_kused, 4 * a + 4)
                            if a == 0:
                                dve.wait_ge(*count_taken("bias"))
                            bias = biasd.rearrange("p (h b j) -> p b j h", h=HEADS, b=NS)[:, a]
                            link(v.tensor_tensor(sc[:, 0:PAGES], sc[:, 0:PAGES], bias, ALU.add))
                            link(v.tensor_copy(sc[:, PAGES], snew[:, a]))
                            v.tensor_reduce(m1, sc.rearrange("p j h -> p h j"), AX.X, ALU.max).then_inc(s_m1, 1)
                    elif step == "dmax":
                        link(v.tensor_reduce(nmax, full("dmax", a)[0:HEADS, 0:P], AX.X, ALU.max, negate=True))
                        v.tensor_scalar(dg, ident8, nmax, None, ALU.mult).then_inc(taken[CHAIN], 1)
                    elif step == "dshift":
                        v.tensor_tensor(sc, sc, full("dshift", a)[:, 0:HEADS].unsqueeze(1).to_broadcast([P, PAGES + 1, HEADS]), ALU.add).then_inc(taken[CHAIN], 1)
                        dve.wait_ge(s_pex, a + 1)
                        v.tensor_reduce(psm, pex[:, :, 0:HEADS].rearrange("p j h -> p h j"), AX.X, ALU.add).then_inc(s_psm, 1)
                    elif step == "dpv":
                        v.reciprocal(rden, full("den", a)[0:NS, 0:1]).then_inc(taken[CHAIN], 1)
                    elif step == "dsum":
                        dve.wait_ge(*count_taken("den", a))
                        if a:
                            dve.wait_ge(*count_full("datt", a - 1))
                        v.scalar_tensor_tensor(mk[0:NS].rearrange("p (h d) -> p h d", h=HEADS),
                                               full("dsum", a)[0:NS, :].rearrange("p (h d) -> p h d", h=HEADS), rden,
                                               ident8.unsqueeze(2).to_broadcast([NS, HEADS, HD]), ALU.mult, ALU.mult).then_inc(taken[SUM], 1)
                    elif step == "datt":
                        v.tensor_copy(attT[:, :, SEQ + a], full("datt", a)[:, 0:CC]).then_inc(taken[CHAIN], 1)
                    elif step == "hnorm":
                            pr = probs[:, a % 2]
                            dve.wait_ge(s_exp, 2 * a + 2)
                            link(v.reciprocal(hinv, hsum))
                            v.tensor_scalar(pr[:, 0:P], pr[:, 0:P], hinv[:, 0:1], None, ALU.mult)
                            v.tensor_scalar(pr[:, P:3 * P], pr[:, P:3 * P], hinv[:, 1:2], None, ALU.mult).then_inc(s_probs, 1)
                    elif step == "head":
                        if a < HEADS:
                            src, pr = full("scores", a), probs[:, a % 2]
                            if a >= 2:
                                dve.wait_ge(*count_full("pT", a - 2))
                            v.scalar_tensor_tensor(pr[:, 0:P], src[:, 0:P], cq[:, 0, a:a + 1], L["mask"][:, P:2 * P], ALU.add, ALU.add)
                            v.scalar_tensor_tensor(pr[:, P:3 * P], src[:, P:3 * P], cq[:, 1, a:a + 1], L["mask"], ALU.add, ALU.add).then_inc(taken[SCORES], 1)
                            dve.wait_ge(*count_taken("scores", a))
                            v.tensor_reduce(hmax[:, 0:1], pr[:, 0:P], AX.X, ALU.max, negate=True)
                            v.tensor_reduce(hmax[:, 1:2], pr[:, P:3 * P], AX.X, ALU.max, negate=True).then_inc(s_rmax, 1)
                    elif step == "pv":
                        r = HD * (a % 2)
                        v.tensor_copy(attT[r:r + HD, a // 2, 0:SEQ], full("pv", a)[r:r + HD, 0:SEQ]).then_inc(taken[TR], 1)
                    elif step == "up":
                        dve.wait_ge(*count_taken("gate", a))
                        v.scalar_tensor_tensor(gates[:, a], gates[:, a], 1.0, full("up", a)[:, 0:TOK], ALU.add, ALU.mult).then_inc(taken[turn["up", a][0]], 1)
                    elif step == "merge":
                        dve.wait_ge(*count_taken("gate", DK + a))
                        dve.wait_ge(*count_taken("up", a))
                        v.scalar_tensor_tensor(gates[:, DK + a], gates[:, DK + a], 1.0, full("merge", a)[:, 0:TOK], ALU.add, ALU.mult).then_inc(taken[turn["merge", a][0]], 1)
                        dve.wait_ge(*count_taken("merge", a))
                        v.tensor_tensor(hT[:, a, 0:TOK], gates[:, a], gates[:, DK + a], ALU.add).then_inc(s_merge, 1)
                    elif step == "out":
                        for half in range(2):
                            xs = x[0:NS, 2, half * 512:(half + 1) * 512]
                            v.scalar_tensor_tensor(xs, full("osum", half)[0:NS], 0.5, xs, ALU.mult, ALU.add).then_inc(taken[SUM], 1)
                            add_out(half)
                    elif step == "norm":
                        dve.wait_ge(s_sq, 5)
                        dve.wait_ge(s_merge, DK)
                        roots(slice(0, 3, 2), P)
                        normalise(2, NS)
                        normalise(0, P)
                        dve.wait_ge(in_route, 16 * 6)
                        add_out(2)
                        add_out(3)
                        for half in range(2):
                            dve.wait_ge(*count_full("opart", half))
                        for i in range(2 * PB):
                            dve.wait_ge(*count_full("out", i))
                        transposed(1, nffn, range(3))
                        dve.wait_ge(s_sq, 6)
                        roots(slice(1, 2), P)
                        normalise(1, P)
                        transposed(1, nffn, range(3, 5))
                    elif step == "route":
                        route()

            def first_of_equals(out, values, top, n, scratch):
                link(v.tensor_reduce(top, values, AX.X, ALU.max))
                link(v.tensor_tensor(scratch, values, top.to_broadcast([P, 3, n]), ALU.is_equal))
                link(v.tensor_tensor(scratch, scratch, L["first"][:, EXPERTS - n:].unsqueeze(1).to_broadcast([P, 3, n]), ALU.mult))
                link(v.tensor_reduce(r_top, scratch, AX.X, ALU.max))
                link(v.tensor_tensor(out, scratch, r_top.to_broadcast([P, 3, n]), ALU.is_equal))

            def route():
                dve.wait_ge(out_pool, 16 * 6)
                v.memset(xg, 0.0).then_inc(s_zero, 1)
                link(v.memset(lgT[0:36], 0.0))
                v.tensor_scalar(lgT[0:36, 0:TOK], full("logits")[0:36, 0:TOK], br[:, 0:1], None, ALU.add).then_inc(taken[PART], 1)
                v.tensor_copy(lg, full("logitsT")[:, 0:3 * 36].rearrange("p (b n) -> p b n", b=3)).then_inc(taken[SUM], 1)
                dve.wait_ge(*count_taken("logitsT"))
                grp = lg[:, :, EXPERTS:]
                first_of_equals(r_oh, grp, r_gm, GROUPS, r_t4)
                v.tensor_tensor(gex, grp, r_gm.to_broadcast([P, 3, GROUPS]), ALU.subtract).then_inc(s_gsh, 1)
                link(v.tensor_scalar(r_oh, r_oh, BIG, -BIG, ALU.mult, ALU.add))
                link(v.tensor_tensor(em.rearrange("p b (g e) -> p b g e", g=GROUPS), lg[:, :, 0:EXPERTS].rearrange("p b (g e) -> p b g e", g=GROUPS),
                                     r_oh.unsqueeze(3).to_broadcast([P, 3, GROUPS, PER_GROUP]), ALU.add))
                first_of_equals(e1, em, r_m1, EXPERTS, ra)
                link(v.scalar_tensor_tensor(em, e1, -2 * BIG, em, ALU.mult, ALU.add))
                first_of_equals(e2, em, r_m2, EXPERTS, ra)
                link(v.tensor_tensor(rr, e1, e2, ALU.add))
                v.tensor_tensor(rr, rr, L["valid"].unsqueeze(2).to_broadcast([P, 3, EXPERTS]), ALU.mult).then_inc(s_rr, 1)
                v.tensor_tensor(tex, r_m2, r_m1, ALU.subtract).then_inc(s_tsh, 1)
                link(v.tensor_copy(rb, full("ranks")[:, 0:96].rearrange("p (b n) -> p b n", b=3)))
                ranks = bank[BIG0]
                for c, e in enumerate((e1, e2)):
                    link(v.tensor_tensor(ra, e, rb, ALU.mult))
                    link(v.tensor_reduce(rank[:, :, c], ra, AX.X, ALU.add))
                    for i in range(2):
                        v.tensor_tensor(selE[:, :, c, i], e, L["pay"].rearrange("p (b c i) -> p b c i", b=3, c=2)[:, :, c, i:i + 1].to_broadcast([P, 3, EXPERTS]), ALU.mult)
                v.tensor_tensor(selS, L["slots"].unsqueeze(1).unsqueeze(1).to_broadcast([P, 3, 2, CAP]),
                                rank.unsqueeze(3).to_broadcast([P, 3, 2, CAP]), ALU.is_equal).then_inc(s_sel, 1)
                v.tensor_scalar(gidx[:].rearrange("p i e -> p (i e)"), full("slots")[:, 0:2 * EXPERTS], 4.0, L["group4"], ALU.mult, ALU.add).then_inc(s_idx, 1)
                for c, e in enumerate((e1, e2)):
                    link(v.tensor_tensor(ra, e, L["expert"].unsqueeze(1).to_broadcast([P, 3, EXPERTS]), ALU.mult))
                    link(v.tensor_reduce(slotpos[:, :, c], ra, AX.X, ALU.add))
                v.scalar_tensor_tensor(posI[:], rank, float(EXPERTS), slotpos, ALU.mult, ALU.add).then_inc(s_pos, 1)
                link(v.tensor_tensor(over.rearrange("p (e j) -> p e j", j=8), ranks[:, 96:128].unsqueeze(2).to_broadcast([P, EXPERTS, 8]),
                                     L["block"].unsqueeze(1).to_broadcast([P, EXPERTS, 8]), ALU.is_gt))
                link(v.memset(ones8, 1.0))
                link(v.tensor_tensor_scan(cs, ones8, over, 0.0, ALU.mult, ALU.add))
                link(v.tensor_scalar(over, cs, L["part"], None, ALU.is_le))
                v.tensor_reduce(lst, over, AX.X, ALU.add).then_inc(s_lst, 1)
                v.tensor_copy(blkI[0:1, 0:1], cs[0:1, 255:256]).then_inc(taken[BIG0], 1)
                link(v.tensor_copy(blkI[0:1, 1:1 + MAXOVER], full("blocks")[0:1, 0:MAXOVER]))
                link(v.tensor_scalar(blkI[0:1, 1 + MAXOVER:], blkI[0:1, 1:1 + MAXOVER], 7, None, ALU.bitwise_and))
                v.tensor_scalar(blkI[0:1, 1:1 + MAXOVER], blkI[0:1, 1:1 + MAXOVER], 3, None, ALU.logical_shift_right).then_inc(taken[CHAIN], 1)
                dve.wait_ge(s_gex, 1)
                link(v.tensor_reduce(r_gs, gex, AX.X, ALU.add))
                dve.wait_ge(s_tex, 1)
                link(v.tensor_scalar(r_ts, tex, 1.0, None, ALU.add))
                link(v.tensor_tensor(r_gs, r_gs, r_ts, ALU.mult))
                link(v.reciprocal(wts[:, 0].unsqueeze(2), r_gs))
                link(v.tensor_tensor(wts[:, 1].unsqueeze(2), wts[:, 0].unsqueeze(2), tex, ALU.mult))

            run_plan()
            nq = nffn[:].rearrange("p (g c) -> p c g", c=2)

            def block_rows(n, p, used):
                dve.wait_ge(s_xt, n + 1)
                for c in range(2):
                    ins = v.tensor_tensor(xgT[:, c], bank[PART][:, c * P:(c + 1) * P].rearrange("p (g s) -> p g s", g=4),
                                          nq[:, c].unsqueeze(2).to_broadcast([P, 4, CAP]), ALU.mult)
                ins.then_inc(s_xgT, 1)
                dve.wait_ge(s_gu, n + 1)
                v.tensor_copy(gu, bank[SUM][:, 0:256]).then_inc(s_gusb, 1)
                dve.wait_ge(s_sg, n + 1)
                v.tensor_tensor(hE, sg, bank[QB][:, 0:256].rearrange("p (c g s) -> p c g s", c=2, g=4)[:, :, 2:4], ALU.mult).then_inc(s_hE, 1)
                dve.wait_ge(s_dn, n + 1)
                if used is not None:
                    dve.wait_ge(s_yst[p], 16 * used)
                v.tensor_copy(ysb[:, p], bank[CHAIN][:, 0:256]).then_inc(s_ysb, 1)

            def later_block(r):
                dve.wait_ge(s_otab, 64 * (r + 1))
                dve.wait_ge(s_icy, r + EXPERTS)
                v.tensor_scalar(oidx[:], otab[:], 4.0, L["group"], ALU.mult, ALU.add).then_inc(s_oidx, 1)
                block_rows(r + EXPERTS, 0, r + EXPERTS // 2)

            for p in range(2):
                block_rows(p, p, None)
            with dve.Fori(1, EXPERTS // 2) as i:
                for p in range(2):
                    block_rows(2 * i + p, p, i)
            later_blocks(dve, later_block)
            v.memset(rowsq[:], 1.0).then_inc(s_pad, 1)
            for i, (b, n) in enumerate(BLOCKS):
                dve.wait_ge(s_yl[i], 16)
                link(v.scalar_tensor_tensor(x[0:n, b], yload[0:n, b, 0], wts[0:n, 0, b:b + 1], x[0:n, b], ALU.mult, ALU.add))
                v.scalar_tensor_tensor(x[0:n, b], yload[0:n, b, 1], wts[0:n, 1, b:b + 1], x[0:n, b], ALU.mult, ALU.add).then_inc(s_x3, 1)
            dve.wait_ge(in_nf, 16)
            dve.wait_ge(s_sq, 9)
            roots(slice(0, 3), P)
            for b, n in BLOCKS:
                v.scalar_tensor_tensor(x[0:n, b], x[0:n, b], root[0:n, b], normf[0:n], ALU.mult, ALU.mult).then_inc(s_fin, 1)

        @block.tensor
        def _(pe):
            m = nc.tensor

            def free(*label):
                b, n = turn[label]
                if n:
                    pe.wait_ge(taken[b], n)
                return bank[b]

            def transposes(which):
                for i, (k, b, half) in enumerate(TPOSE):
                    out = free("hT", which, i)
                    pe.wait_ge(s_h, 3 * which + (1, 2, 3)[(2, 0, 1).index(b)])
                    if b == 2:
                        for c in range(DK):
                            last = m.transpose(out[:, c * NS:(c + 1) * NS], h[0:NS, 2, c * P:(c + 1) * P], ident8)
                    else:
                        for c in range(4):
                            last = m.transpose(out[:, c * P:(c + 1) * P], h[:, b, (4 * half + c) * P:(4 * half + c + 1) * P], ident)
                    last.then_inc(filled[k], 1)

            pe.wait_ge(in_ce, 16)
            transposes(0)
            pe.wait_ge(s_pad, 3)
            for i in range(len(TPOSE)):
                pe.wait_ge(*count_taken("hT", 0, i))

            for step, a in PLAN:
                if step == "proj":
                    w = wait_loaded(pe, "w", a).rearrange("p (k n) -> p k n", k=DK)
                    out = free("part", a)
                    for k in range(DK):
                        g = 32 * (k % 4)
                        last = m.matmul(out[g:g + 32, :], hT[:, k, SEQ:TPAD], w[:, k], start=k < 4, stop=k >= 4)
                    last.then_inc(filled[PART], 1)
                    for b in range(PB):
                        out = free("proj", a, b)
                        for k in range(DK):
                            last = m.matmul(out[:], hT[:, k, b * P:(b + 1) * P], w[:, k], start=k == 0, stop=k == DK - 1)
                        last.then_inc(filled[turn["proj", a, b][0]], 1)
                        if b == 0:
                            out = free("sum", a)
                            pe.wait_ge(*count_taken("part", a))
                            m.matmul(out[0:NS, :], E["sum8"], part[:], start=True, stop=True).then_inc(filled[SUM], 1)
                elif step == "forget":
                    out = free("forget")
                    pe.wait_ge(in_wf, 32)
                    for k in range(DK):
                        last = m.matmul(out[0:HEADS, 0:TOK], wf[:, k], hT[:, k, 0:TOK], start=k == 0, stop=k == DK - 1)
                    last.then_inc(filled[CHAIN], 1)
                elif step == "forgetT":
                    out = free("forgetT")
                    pe.wait_ge(s_lf, 1)
                    for b in range(PB):
                        m.transpose(out[:, 8 * b:8 * b + 8], cneg[:, b * P:(b + 1) * P], ident8)
                        m.transpose(out[:, 16 + 8 * b:24 + 8 * b], lf8[:, b * P:(b + 1) * P], ident8)
                    m.transpose(out[0:NS, 32:40], lf8[:, SEQ:TOK], ident8).then_inc(filled[CHAIN], 1)
                elif step == "pages":
                    out = free("pagesT")
                    pe.wait_ge(in_lfp, 16)
                    rows = lfp[0:NS * PAGES].rearrange("p (r h) -> p h r", h=HEADS)
                    for hh in range(HEADS):
                        last = m.transpose(out[:, 64 * hh:64 * hh + 64], rows[:, hh], ident[0:64, 0:64])
                    last.then_inc(filled[SCORES], 1)
                elif step == "bias":
                    out = free("bias")
                    pe.wait_ge(in_cl, 16)
                    pe.wait_ge(s_lfd, 1)
                    m.matmul(out[:], L["later"], lfT, start=True, stop=False)
                    m.matmul(out[:], ones, lfC, start=False, stop=False)
                    m.matmul(out[:], ones[0:NS], lfd[0:NS], start=False, stop=True).then_inc(filled[SCORES], 1)
                elif step == "qk":
                    c0, b = (C_Q, C_K)[a // 2], a % 2
                    out = free("qk", a)
                    pe.wait_ge(*count_taken("proj", c0, b))
                    for c in range(CC):
                        last = m.transpose(out[:, c * P:(c + 1) * P], tok[:, b, c0, c * P:(c + 1) * P], ident)
                    last.then_inc(filled[turn["qk", a][0]], 1)
                elif step == "dq":
                    out = free("dq", a)
                    pe.wait_ge(*count_taken("sum", C_Q))
                    m.matmul(out[:], ident8[:, a:a + 1].to_broadcast([NS, P]), samp[0:NS, C_Q], start=True, stop=True).then_inc(filled[QB], 1)
                elif step == "dmax":
                    out = free("dmax", a)
                    pe.wait_ge(s_m1, a + 1)
                    m.transpose(out[0:HEADS, 0:P], m1, ident).then_inc(filled[CHAIN], 1)
                elif step == "dshift":
                    out = free("dshift", a)
                    m.matmul(out[:, 0:HEADS], ones[0:HEADS], dg, start=True, stop=True).then_inc(filled[CHAIN], 1)
                elif step == "dpv":
                    out = free("dpv", a)
                    pe.wait_ge(s_pex, a + 1)
                    pages = wait_loaded(pe, "V", a).rearrange("p (j n) -> p j n", j=PAGES)
                    for j in range(PAGES):
                        g = 32 * (j % 4)
                        m.matmul(out[g:g + 32, :], pex[:, j], pages[:, j], start=j < 4, stop=j >= 4 and j % 4 > 0)
                    m.matmul(out[0:32, :], pex[0:NS, PAGES], samp[0:NS, C_V], start=False, stop=True).then_inc(filled[PART], 1)
                    out = free("den", a)
                    pe.wait_ge(s_psm, a + 1)
                    m.matmul(out[0:HEADS, 0:1], psm, ones[:, 0:1], start=True, stop=True).then_inc(filled[CHAIN], 1)
                elif step == "dsum":
                    out = free("dsum", a)
                    pe.wait_ge(*count_taken("dpv", a))
                    m.matmul(out[0:NS, :], E["sum8"], part[:], start=True, stop=True).then_inc(filled[SUM], 1)
                elif step == "datt":
                    out = free("datt", a)
                    pe.wait_ge(*count_taken("dsum", a))
                    for c in range(CC):
                        last = m.matmul(out[:, c:c + 1], mk[0:NS, c * P:(c + 1) * P], ones[0:NS, 0:1], start=True, stop=True)
                    last.then_inc(filled[CHAIN], 1)
                elif step == "pool":
                    if a < CC:
                        out = free("pool", a)
                        if a == 0:
                            pe.wait_ge(in_pool, 16 * 4)
                            for b in range(PB):
                                pe.wait_ge(*count_taken("proj", C_U, b))
                            pe.wait_ge(*count_taken("sum", C_U))
                        cols = slice(a * P, (a + 1) * P)
                        m.matmul(out[:, 0:P], tok[:, 0, C_U, cols], C["first"][:, a], start=True, stop=True)
                        m.matmul(out[:, P:SEQ], tok[:, 1, C_U, cols], C["full"][:, a], start=True, stop=False)
                        m.matmul(out[:, P:P + PLEN], tok[:, 0, C_U, cols], C["before"][:, a], start=False, stop=True)
                        m.matmul(out[:, SEQ:TOK], state[0:NS * PLEN, cols], C["state"][0:NS * PLEN, a], start=True, stop=False)
                        m.matmul(out[:, SEQ:TOK], samp[0:NS, C_U, cols], C["mine"][0:NS, a], start=False, stop=True).then_inc(filled[turn["pool", a][0]], 1)
                    if a:
                        out = free("mix", a - 1)
                        pe.wait_ge(*count_taken("pool", a - 1))
                        m.matmul(out[:, 0:TOK], wpool[:, a - 1], pooledT[:, (a - 1) % 2], start=True, stop=True).then_inc(filled[turn["mix", a - 1][0]], 1)
                elif step == "gate":
                    w = wait_loaded(pe, "g", a // GPS).rearrange("p (k n) -> p k n", k=DK)
                    out = free("gate", a)
                    cols = slice((a % GPS) * P, (a % GPS + 1) * P)
                    for k in range(DK):
                        last = m.matmul(out[:, 0:TOK], w[:, k, cols], hT[:, k, 0:TOK], start=k == 0, stop=k == DK - 1)
                    last.then_inc(filled[turn["gate", a][0]], 1)
                elif step == "head":
                    if a:
                        out = free("pT", a - 1)
                        pe.wait_ge(s_probs, a)
                        pr = probs[:, (a - 1) % 2]
                        for i in range(3):
                            last = m.transpose(out[:, i * P:(i + 1) * P], pr[:, i * P:(i + 1) * P], ident)
                        last.then_inc(filled[TR], 1)
                    if a < HEADS:
                        out = free("scores", a)
                        if a == 0:
                            for i in range(4):
                                pe.wait_ge(*count_taken("qk", i))
                        r, c = slice(HD * (a % 2), HD * (a % 2) + HD), a // 2
                        onehot = ident8[:, a:a + 1].to_broadcast([NS, P])
                        for b, cols in ((0, slice(0, P)), (1, slice(P, 3 * P))):
                            n = (b + 1) * P
                            m.matmul(out[:, cols], qT[r, c, b * P:(b + 1) * P], kT[r, c, 0:n], start=True, stop=False)
                            last = m.matmul(out[:, cols], onehot, cneg[:, 0:n], start=False, stop=True)
                        last.then_inc(filled[SCORES], 1)
                elif step == "pv":
                    out = free("pv", a)
                    hd = slice(a * HD, (a + 1) * HD)
                    r = slice(HD * (a % 2), HD * (a % 2) + HD)
                    m.matmul(out[r, 0:P], tok[:, 0, C_V, hd], probsT[:, 0:P], start=True, stop=True)
                    m.matmul(out[r, P:SEQ], tok[:, 0, C_V, hd], probsT[:, P:2 * P], start=True, stop=False)
                    m.matmul(out[r, P:SEQ], tok[:, 1, C_V, hd], probsT[:, 2 * P:3 * P], start=False, stop=True).then_inc(filled[TR], 1)
                elif step in ("up", "merge"):
                    w = wait_loaded(pe, "up", int(step == "merge")).rearrange("p (k n) -> p k n", k=CC)
                    out = free(step, a)
                    if a == 0 and step == "up":
                        pe.wait_ge(*count_taken("mix", CC - 1))
                    if a == 0 and step == "merge":
                        pe.wait_ge(*count_taken("datt", NS - 1))
                        pe.wait_ge(*count_taken("pv", HEADS - 1))
                    src = mixedT if step == "up" else attT
                    for k in range(CC):
                        last = m.matmul(out[:, 0:TOK], w[:, k, a * P:(a + 1) * P], src[:, k], start=k == 0, stop=k == CC - 1)
                    last.then_inc(filled[turn[step, a][0]], 1)
                elif step == "out":
                    w = [wait_loaded(pe, "out", i).rearrange("p (k n) -> p k n", k=CC) for i in range(2)]
                    pe.wait_ge(s_merge, DK)
                    for half in range(2):
                        out = free("opart", half)
                        for k in range(DK):
                            g = 32 * (k % 4)
                            last = m.matmul(out[g:g + 32, :], hT[:, k, SEQ:TPAD], w[k // CC][:, k % CC, half * 512:(half + 1) * 512], start=k < 4, stop=k >= 4)
                        last.then_inc(filled[turn["opart", half][0]], 1)
                    for i in range(2 * PB):
                        out = free("out", i)
                        b, half = i // 2, i % 2
                        for k in range(DK):
                            last = m.matmul(out[:], hT[:, k, b * P:(b + 1) * P], w[k // CC][:, k % CC, half * 512:(half + 1) * 512], start=k == 0, stop=k == DK - 1)
                        last.then_inc(filled[turn["out", i][0]], 1)
                        if i < 2:
                            out = free("osum", i)
                            pe.wait_ge(*count_taken("opart", i))
                            m.matmul(out[0:NS, :], E["sum8"], part[:], start=True, stop=True).then_inc(filled[SUM], 1)
                elif step == "norm":
                    transposes(1)
                elif step == "route":
                    out = free("logits")
                    pe.wait_ge(s_wr, 2)
                    for i in range(len(TPOSE)):
                        pe.wait_ge(*count_taken("hT", 1, i))
                    for k in range(DK):
                        last = m.matmul(out[0:36, 0:TOK], wr[:, k], hT[:, k, 0:TOK], start=k == 0, stop=k == DK - 1)
                    last.then_inc(filled[PART], 1)
                    out = free("logitsT")
                    pe.wait_ge(*count_taken("logits"))
                    for b in range(3):
                        last = m.transpose(out[:, 36 * b:36 * b + 36], lgT[0:36, b * P:(b + 1) * P], ident[0:36, 0:36])
                    last.then_inc(filled[SUM], 1)
                    out = free("ranks")
                    pe.wait_ge(s_rr, 1)
                    for b in range(3):
                        for c in range(b + 1):
                            m.matmul(out[:, 32 * b:32 * b + 32], L["earlier"] if c == b else ones, rr[:, c], start=c == 0, stop=c == b)
                    for c in range(3):
                        last = m.matmul(out[:, 96:128], ones, rr[:, c], start=c == 0, stop=c == 2)
                    last.then_inc(filled[BIG0], 1)
                    out = free("slots")
                    pe.wait_ge(s_sel, 1)
                    pairs = [(b, c) for b in range(3) for c in range(2)]
                    for q in range(4):
                        for b, c in pairs:
                            last = m.matmul(out[CAP * q:CAP * (q + 1), 0:2 * EXPERTS], selS[:, b, c], selE[:, b, c].rearrange("p i e -> p (i e)"),
                                            start=(b, c) == pairs[0], stop=(b, c) == pairs[-1])
                    last.then_inc(filled[BIG1], 1)
                    out = free("blocks")
                    pe.wait_ge(s_lst, 1)
                    m.matmul(out[0:1, 0:MAXOVER], lst, ident[:, 0:MAXOVER], start=True, stop=True).then_inc(filled[CHAIN], 1)

            def expert(e, p, used, q, in_slots):
                pe.wait_ge(s_xg[p], 16 * used + 16)
                for c in range(2):
                    last = m.transpose(bank[PART][:, c * P:(c + 1) * P], xg[:, p, c * P:(c + 1) * P], ident)
                last.then_inc(s_xt, 1)
                pe.wait_ge(s_xgT, e + 1)
                pe.wait_ge(s_slot[q], in_slots[0])
                pe.wait_ge(s_slot[q + 1], in_slots[1])
                for k in range(DK):
                    for g in range(4):
                        w = slot[q + g // 2].rearrange("p (k n) -> p k n", k=DK)
                        last = m.matmul(bank[SUM][32 * g:32 * g + 32, 0:256], xgT[:, k % 2, k // 2], w[:, k, 256 * (g % 2):256 * (g % 2) + 256],
                                        start=k == 0, stop=k == DK - 1)
                last.then_inc(s_gu, 1)
                pe.wait_ge(s_gusb, e + 1)
                for c in range(2):
                    last = m.transpose(bank[QB][:, c * P:(c + 1) * P], gu[:, c * P:(c + 1) * P], ident)
                last.then_inc(s_guT, 1)
                pe.wait_ge(s_hE, e + 1)
                pe.wait_ge(s_slot[q + 2], in_slots[2])
                wd = slot[q + 2].rearrange("p (k n) -> p k n", k=FC)
                for j in range(FC):
                    for g in range(4):
                        last = m.matmul(bank[CHAIN][32 * g:32 * g + 32, 0:256], hE[:, j % 2, j // 2], wd[:, j, 256 * g:256 * g + 256],
                                        start=j == 0, stop=j == FC - 1)
                last.then_inc(s_dn, 1)

            for b, lab in ((QB, ("hT", 1, 0)), (CHAIN, ("blocks",)), (SUM, ("logitsT",)), (PART, ("logits",))):
                pe.wait_ge(*count_taken(*lab))
            with pe.Fori(0, EXPERTS // 6) as i:
                for r in range(6):
                    q = 3 * (r % 3)
                    expert(6 * i + r, r % 2, 3 * i + r // 2, q, [32 * i + (SLOT_BASE[q + m] + 16 * (r // 3 + 1)) for m in range(3)])
            for e in range(EXPERTS // 6 * 6, EXPERTS):
                q = 3 * (e % 3)
                expert(e, e % 2, e // 2, q, [SLOT_BASE[q + m] + 16 * (e // 3 + 1) for m in range(3)])
            later_blocks(pe, lambda r: expert(r + EXPERTS, 0, r + EXPERTS // 2, 0, [16 * r + (AFTER[m] + 16) for m in range(3)]))


_INS = ["x_prompt", "x_sample", "cache_k", "cache_v", "cache_logf", "state_pool", "page_table", "norm_mix", "w_in", "b_forget",
        "w_pool", "pool_scale", "w_up_pool", "w_up_att", "w_out", "norm_ffn", "w_router_group", "b_router_group",
        "w_router_expert", "b_router_expert", "w_gate", "w_up", "w_down", "norm_final"]
_OUTS = [("y_prompt", (1, SEQ, D)), ("y_sample", (NS, 1, D)), ("new_k_prompt", (1, 1, SEQ, HEADS, HD)), ("new_v_prompt", (1, 1, SEQ, HEADS, HD)),
         ("new_logf_prompt", (1, 1, SEQ, HEADS)), ("new_pool_prompt", (1, 1, PLEN, DC)), ("new_k_sample", (1, NS, 1, HEADS, HD)),
         ("new_v_sample", (1, NS, 1, HEADS, HD)), ("new_logf_sample", (1, NS, 1, HEADS)), ("new_pool_sample", (1, NS, PLEN, DC))]


def kernel(**inputs):
    from concourse import bacc
    from concourse.bass_utils import run_bass_kernel_spmd

    early, late, poolc, payload = constants()
    arrays = {name: np.ascontiguousarray(inputs[name]) for name in _INS}
    for name, parts in (("c_early", early), ("c_late", late), ("c_pool", poolc)):
        arrays[name] = np.ascontiguousarray(np.concatenate([np.asarray(a, np.float32) for a in parts.values()], 1))
    arrays["c_pay"] = payload
    nc = bacc.Bacc("TRN2", target_bir_lowering=False, num_devices=1)
    t = {name: nc.dram_tensor(name, a.shape, mybir.dt.from_np(a.dtype), kind="ExternalInput").ap() for name, a in arrays.items()}
    for name, shape in _OUTS:
        t[name] = nc.dram_tensor(name, shape, F32, kind="ExternalOutput").ap()
    build(nc, t)
    r = run_bass_kernel_spmd(nc, [arrays], core_ids=[0])
    return tuple(r.results[0][name] for name, _ in _OUTS)
```

```python
import numpy as np
import concourse.bass as bass
from concourse import mybir
from contextlib import ExitStack

F32 = mybir.dt.float32
I32 = mybir.dt.int32
ALU = mybir.AluOpType
ACT = mybir.ActivationFunctionType
AX = mybir.AxisListType

P = 128
D = 1024
DK = D // P
SEQ = 256
PB = SEQ // P
NS = 8
TOK = SEQ + NS
TPAD = SEQ + 32
HEADS, HD = 8, 64
DC = HEADS * HD
CC = DC // P
PAGES = 8
NPHYS = 80
WINDOWS = (2, 4, 8, 16)
PLEN = 15
GROUPS, PER_GROUP = 4, 8
EXPERTS = GROUPS * PER_GROUP
FE = 512
FC = FE // P
EPS = 1e-6
QSCALE = HD ** -0.5
BIG = 1e30
C_U, C_Q, C_K, C_V = 0, 1, 2, 3
W_FORGET = 4 * DC
W_GATE = W_FORGET + HEADS
NT = 2 * DK
GPS = DC // P

CAP = 32
RANKS = 288
MAXOVER = 2 * TOK // CAP
NONE = 65536
SLOT = 4096
NSLOT = 9
NB = NSLOT // 3
FRONT = 6


def band(w):
    s, t = np.arange(P)[:, None], np.arange(P)[None, :]
    inside = (t >= s) & (t - s < w)
    own = (s == t).astype(np.float64)
    first = inside / np.minimum(t + 1, w) - own
    full = inside / w - own
    before = ((t + P - s) < w)[:, :PLEN] / w
    state = np.zeros((P, NS))
    for b in range(NS):
        for j in range(PLEN - (w - 1), PLEN):
            state[b * PLEN + j, b] = 1 / w
    mine = np.zeros((P, NS))
    mine[:NS] = np.eye(NS) * (1 / w - 1)
    return first, full, before, state, mine


def constants():
    s, t = np.arange(P)[:, None], np.arange(P)[None, :]
    p = np.arange(P)
    sum8 = np.zeros((P, NS))
    for g in range(4):
        sum8[32 * g:32 * g + NS] = np.eye(NS)
    early = {
        "ident": np.eye(P),
        "sum8": sum8,
    }
    mask = np.zeros((P, 2 * P))
    mask[:, P:] = np.where(t <= s, 0.0, -BIG)
    other = np.zeros((P, NS))
    other[:NS] = np.where(np.eye(NS) > 0, 0.0, -BIG)
    valid = np.ones((P, 3))
    valid[NS:, 2] = 0
    token = (np.arange(3)[None, :, None] * P + p[:, None, None]) + np.zeros((1, 1, 2))
    pay = np.stack([token, 2 * token + np.arange(2)[None, None, :]], -1)
    late = {
        "later": (s > t),
        "earlier": (s < t),
        "ones": np.ones((P, P)),
        "mask": mask,
        "other": other,
        "valid": valid,
        "first": np.tile(np.arange(EXPERTS, 0, -1.0), (P, 1)),
        "expert": np.tile(np.arange(EXPERTS) * 1.0, (P, 1)),
        "block": np.tile(np.arange(1, 9) * float(CAP), (P, 1)),
        "group": (p // 32)[:, None] * 1.0,
        "part": p[:, None] * 1.0,
        "own": (p[:, None] % 32 == np.arange(HEADS)[None, :]) * 1.0,
        "slots": np.tile(np.arange(CAP) * 1.0, (P, 1)),
        "group4": (p // 32)[:, None] + 4.0 * NONE,
        "pay": np.where((token < TOK)[..., None], pay - 1.0 * NONE, 0.0).reshape(P, 12),
    }
    bands = [band(w) for w in WINDOWS]
    pool = {name: np.concatenate([b[i] for b in bands], 1)
            for i, name in enumerate(("first", "full", "before", "state", "mine"))}
    return early, late, pool, pay.reshape(P, 12).astype(np.int32)


def columns(parts):
    at, out = 0, {}
    for name, a in parts.items():
        out[name] = (at, at + a.shape[1])
        at += a.shape[1]
    return out, at


def build(nc, t):
    early, late, poolc, _ = constants()
    (ce, ne), (cl, nl), (cp, np_) = columns(early), columns(late), columns(poolc)
    ctx = ExitStack()
    with ctx:
        def sb(name, shape, dt=F32):
            return ctx.enter_context(nc.sbuf_tensor(name, shape, dt))

        def sem(name):
            return ctx.enter_context(nc.semaphore(name))

        ring = sb("ring", [P, NSLOT * SLOT + P])
        slot = [ring[:, n * SLOT:(n + 1) * SLOT] for n in range(NSLOT)]
        tok = slot[6].rearrange("p (b c n) -> p b c n", b=PB, c=4)
        qT = slot[7][:, 0:1024].rearrange("p (c n) -> p c n", c=CC)
        kT = slot[7][:, 1024:2048].rearrange("p (c n) -> p c n", c=CC)
        attT = slot[7][:, 2048:2048 + CC * TOK].rearrange("p (c n) -> p c n", c=CC)
        end8 = ring[:, 8 * SLOT:]
        h = end8[:, 0:3 * D].rearrange("p (b n) -> p b n", b=3)
        lfp = end8[:, 3 * D:4 * D]
        lfT = end8[:, 3 * D:3 * D + 512]
        lfC = end8[:, 3 * D + 512:4 * D]
        gates = end8[:, 0:NT * TOK].rearrange("p (n t) -> p n t", n=NT)
        yload = ring[:, 6 * SLOT:9 * SLOT].rearrange("p (b c n) -> p b c n", b=6, c=2)[:, 0:3]

        x = sb("x", [P, 3, D])
        hT = sb("hT", [P, DK, TPAD])
        cea = sb("cea", [P, ne])
        cla = sb("cla", [P, nl])
        E = {n: cea[:, a:b] for n, (a, b) in ce.items()}
        L = {n: cla[:, a:b] for n, (a, b) in cl.items()}
        ident = E["ident"]
        nmix = sb("nmix", [P, DK])
        nffn = sb("nffn", [P, DK])
        pay = sb("pay", [P, 12], I32)
        wf = sb("wf", [P, DK, HEADS])
        wre = sb("wre", [P, GROUPS, DK * PER_GROUP])
        wrg = sb("wrg", [P, DK * GROUPS])
        wr = sb("wr", [P, DK, EXPERTS + GROUPS])
        br = sb("br", [EXPERTS + GROUPS, 1])
        bf = sb("bf", [HEADS, 1])
        pscale = sb("pscale", [P, CC])
        ptab = sb("ptab", [1, NS * PAGES], I32)
        pidx = sb("pidx", [NS * PAGES, 1], I32)
        part = sb("part", [P, DC])
        stat = sb("stat", [P, 32])
        hmax, hsum, hinv = stat[:, 0:2], stat[:, 2:4], stat[:, 4:6]
        nmax, rden, dsc = stat[0:NS, 6:7], stat[:, 7:8], stat[:, 8:16]
        rowsq = sb("rowsq", [P, 3, 1])
        root = sb("root", [P, 3, 1])
        rowt = sb("rowt", [P, 3, 1])

        NFRONT = 8280
        front = sb("front", [P, NFRONT])
        at = [0]

        def carve(n, base=None):
            if base is not None:
                at[0] = base
            at[0] += n
            assert at[0] <= NFRONT, at[0]
            return front[:, at[0] - n:at[0]]

        samp = carve(4 * DC, 0).rearrange("p (c n) -> p c n", c=4)
        qb = carve(2 * DC).rearrange("p (i n) -> p i n", i=2)
        biasd = carve(DC)
        pooledT = carve(2 * TOK).rearrange("p (i n) -> p i n", i=2)
        mixedT = carve(CC * TOK).rearrange("p (c n) -> p c n", c=CC)
        probs_all = carve(9 * P)
        probs = probs_all[:, 0:6 * P].rearrange("p (i n) -> p i n", i=2)
        probsT = probs_all[:, 6 * P:]
        cpa = end8[:, 0:np_]
        state = end8[:, np_:np_ + DC]
        wpool = end8[:, np_ + DC:np_ + DC + CC * P].rearrange("p (g n) -> p g n", g=CC)
        C = {n: cpa[:, a:b].rearrange("p (g n) -> p g n", g=CC) for n, (a, b) in cp.items()}
        lfd = carve(DC)
        f_ln = lfd[0:HEADS, 0:TOK]
        lf8 = pooledT[0:HEADS, 0]
        cneg = carve(SEQ)[0:HEADS]
        f_z, f_e, f_w, f_min = (probs_all[0:HEADS, i * TOK:(i + 1) * TOK] for i in range(4))
        cq = carve(PB * HEADS).rearrange("p (b n) -> p b n", b=PB)
        lft = carve(3 * HEADS).rearrange("p (b n) -> p b n", b=3)
        snew = carve(NS * HEADS).rearrange("p (b n) -> p b n", b=NS)
        scs = carve(2 * 9 * HEADS).rearrange("p (i j n) -> p i j n", i=2, j=9)
        pex = carve(9 * 32).rearrange("p (j n) -> p j n", j=9)
        m1 = carve(HEADS)
        psm = carve(P)
        dg = carve(HEADS)[0:HEADS]
        mk = carve(DC)
        qs = mk[0:NS]
        sqout = mixedT.rearrange("p c n -> p (c n)")[:, 0:D]

        xg = carve(NB * 256, 0).rearrange("p (i n) -> p i n", i=NB)
        xgT = carve(256).rearrange("p (c g s) -> p c g s", c=2, g=4)
        gu = carve(256)
        sg = carve(P).rearrange("p (c g s) -> p c g s", c=2, g=2)
        hE = carve(P).rearrange("p (c g s) -> p c g s", c=2, g=2)
        ysb = carve(NB * 256).rearrange("p (i n) -> p i n", i=NB)
        normf = carve(D)
        lgT = carve(3 * P)
        lg = carve(3 * 36).rearrange("p (b n) -> p b n", b=3)
        ra = carve(3 * 32).rearrange("p (b n) -> p b n", b=3)
        rb = carve(3 * 32).rearrange("p (b n) -> p b n", b=3)
        em = carve(3 * 32).rearrange("p (b n) -> p b n", b=3)
        e1 = carve(3 * 32).rearrange("p (b n) -> p b n", b=3)
        e2 = carve(3 * 32).rearrange("p (b n) -> p b n", b=3)
        rr = carve(3 * 32).rearrange("p (b n) -> p b n", b=3)
        cs = carve(256)
        over = carve(256)
        ones8 = carve(256)
        sqend = carve(D)
        r_gm, r_m1, r_m2, r_top, r_gs, r_ts, tex = (carve(3).unsqueeze(2) for _ in range(7))
        r_oh, r_t4, gex = (carve(3 * GROUPS).rearrange("p (b n) -> p b n", b=3) for _ in range(3))
        slotpos = carve(6).rearrange("p (b c) -> p b c", b=3)
        rank = carve(6).rearrange("p (b c) -> p b c", b=3)
        selE = carve(3 * 2 * 2 * EXPERTS).rearrange("p (b c i e) -> p b c i e", b=3, c=2, i=2)
        selS = carve(3 * 2 * CAP).rearrange("p (b c s) -> p b c s", b=3, c=2)
        lst = carve(1)

        wts = sb("wts", [P, 2, 3])
        posI = sb("posI", [P, 3, 2], I32)
        gidx = sb("gidx", [P, 2, EXPERTS], I32)
        small = sb("small", [P, 5 + 2 * NB], I32)
        otab, oidx, zeroI = small[:, 0:2], small[:, 2:4], small[:, 4:5]
        icolg, icoly = small[:, 5:5 + NB], small[:, 5 + NB:]
        blkI = sb("blkI", [1, 1 + 2 * MAXOVER], I32)
        none = part[:, 0:RANKS * EXPERTS * 2 // P].bitcast(I32)

        bank = [ctx.enter_context(nc.psum_tensor(f"bank{i}", [P, 512], F32)) for i in range(8)]
        BIG0, BIG1, PART, SUM, QB, CHAIN, SCORES, TR = range(8)
        filled = [sem(f"bank{i}_filled") for i in range(8)]
        taken = [sem(f"bank{i}_taken") for i in range(8)]

        hs = nc.dram_tensor("h_scratch", [TOK * 4, 256], F32).ap()
        qd = nc.dram_tensor("q_scratch", [NS, DC], F32).ap()
        ys = nc.dram_tensor("y_scratch", [TOK * 2 * 4, 256], F32).ap()
        table = nc.dram_tensor("slot_table", [RANKS * EXPERTS, 2], I32).ap()

        PLAN = [("proj", C_Q), ("dq", 0), ("dq", 1), ("proj", C_K), ("forget", 0), ("proj", C_V), ("forgetT", 0), ("pages", 0),
                ("keys0", 0), ("keys1", 0)] + [("qk", i) for i in range(4)] + [
                ("proj", C_U), ("keys2", 0), ("bias", 0), ("keys3", 0), ("pool", 0), ("dmax", 0)]
        PLAN += [("pool", g) for g in range(1, CC + 1)]
        for b in range(1, NS + 1):
            now = b < NS
            PLAN += [("hnorm", b - 2)] * (b > 1) + [("dq", b + 1)] * (b + 1 < NS) + [("keys0", b)] * now
            PLAN += [("gate", 2 * b - 2), ("dshift", b - 1)] + [("keys1", b)] * now + [("dsums", b - 1), ("head", b - 1), ("dpv", b - 1)]
            PLAN += [("keys2", b)] * now + [("dsum", b - 1), ("gate", 2 * b - 1)] + [("keys3", b)] * now
            PLAN += [("datt", b - 1)] + [("up", b - 1), ("dmax", b)] * now + [("pv", b - 2)] * (b > 1)
        PLAN += [("hnorm", HEADS - 1), ("head", HEADS), ("up", DK - 1), ("pv", HEADS - 1)]
        PLAN += [("merge", n) for n in range(DK)] + [("out", 0), ("norm", 0), ("route", 0)]

        uses = {("w", c): (("proj", c), ("proj", c)) for c in range(4)}
        uses.update({("g", n): (("gate", GPS * n), ("gate", GPS * n + GPS - 1)) for n in range(4)})
        for b in range(NS):
            uses["K", b] = ("keys0", b), ("keys3", b)
            uses["V", b] = ("dpv", b), ("dpv", b)
        uses["up", 0] = ("up", 0), ("up", DK - 1)
        uses["up", 1] = ("merge", 0), ("merge", DK - 1)
        uses["out", 0] = uses["out", 1] = ("out", 0), ("out", 0)
        STREAM = sorted(uses, key=lambda item: PLAN.index(uses[item][0]))
        last_step, where, before = [-1] * FRONT, {}, {}
        for item in STREAM:
            q = last_step.index(min(last_step))
            before[item] = [i for i in where if where[i] == q][-1:]
            where[item], last_step[q] = q, PLAN.index(uses[item][1])
        loaded, slot_count = {}, [0] * NSLOT
        for item in STREAM:
            slot_count[where[item]] += 16 * (PAGES if item[0] in "KV" else 1)
            loaded[item] = slot_count[where[item]]
        SLOT_BASE = list(slot_count)
        last_step += [PLAN.index(("pv", HEADS - 1)), PLAN.index(("merge", DK - 1)), len(PLAN)]
        FREED = sorted(range(NSLOT), key=lambda q: last_step[q])

        turn, fills, big = {}, [0] * 8, [0]

        def assign(b, *label):
            if b is None:
                b = (BIG0, BIG1)[big[0] % 2]
                big[0] += 1
            turn[label] = (b, fills[b])
            fills[b] += 1

        TPOSE = [(QB, 2, 0), (BIG0, 0, 0), (BIG1, 0, 1), (SCORES, 1, 0), (TR, 1, 1)]
        for i, (b, _, _) in enumerate(TPOSE):
            assign(b, "hT", 0, i)
        for step, a in PLAN:
            if step == "proj":
                assign(PART, "part", a), assign(SUM, "sum", a), assign(None, "proj", a, 0), assign(None, "proj", a, 1)
            elif step == "forget":
                assign(CHAIN, "forget")
            elif step == "forgetT":
                assign(CHAIN, "forgetT")
            elif step == "pages":
                assign(SCORES, "pagesT")
            elif step == "bias":
                assign(SCORES, "bias")
            elif step == "qk":
                assign((TR, SCORES)[a % 2], "qk", a)
            elif step in ("dmax", "dshift", "datt"):
                assign(CHAIN, step, a)
            elif step == "dpv":
                assign(PART, "dpv", a), assign(CHAIN, "den", a)
            elif step == "pool":
                if a < CC:
                    assign(None, "pool", a)
                if a:
                    assign(None, "mix", a - 1)
            elif step in ("gate", "up", "merge"):
                assign(None, step, a)
            elif step == "head":
                if a < HEADS:
                    assign(SCORES, "scores", a)
                if a:
                    assign(TR, "pT", a - 1)
            elif step == "pv":
                assign(TR, "pv", a)
            elif step == "out":
                for half in range(2):
                    assign((PART, QB)[half], "opart", half), assign(SUM, "osum", half)
                for i in range(4):
                    assign((BIG0, BIG1, SCORES, TR)[i], "out", i)
            elif step == "norm":
                for i, (b, _, _) in enumerate(TPOSE):
                    assign(b, "hT", 1, i)
            elif step == "route":
                assign(PART, "logits"), assign(SUM, "logitsT"), assign(BIG0, "ranks"), assign(BIG1, "slots"), assign(SCORES, "totals"), assign(CHAIN, "blocks")

        s_slot = [sem(f"slot{i}_loaded") for i in range(NSLOT)]
        in_xs, in_xp, in_ce, in_cl, in_nm, in_wf, in_ptab, in_pidx, in_pool, in_route, in_nf, in_lfp = (
            sem(n) for n in ("x_sample_in", "x_prompt_in", "early_consts_in", "late_consts_in", "norm_mix_in", "forget_weights_in",
                             "page_table_in", "page_index_in", "pool_weights_in", "router_in", "norm_final_in", "page_forgets_in"))
        out_tok, out_pool, out_y = sem("prompt_rows_written"), sem("outputs_written_by_pool"), sem("y_written")
        l_dve = sem("dve_link")
        s_sq, l_act, s_h, s_pad = sem("mean_squares_ready"), sem("act_link"), sem("rows_normalised"), sem("pads_set")
        s_fz, s_fexp, s_fw, s_fln, s_lf, s_lfd = (sem(n) for n in (
            "forget_logits_ready", "forget_exp", "forget_exp_plus_one", "forget_ln", "log_forget_ready", "page_forgets_summed"))
        s_kused, s_m1, s_pex, s_psm = (sem(n) for n in (
            "K_slots_used", "page_max_ready", "decode_probs_ready", "prob_sums_ready"))
        s_kprod, s_qs, s_qd = sem("key_products_ready"), sem("queries_scaled"), sem("queries_written")
        s_qb = [sem(f"query_broadcast{i}") for i in range(2)]
        s_rmax, s_exp, s_probs, s_merge = sem("row_max_ready"), sem("prompt_exp_ready"), sem("probs_ready"), sem("branches_merged")
        s_hs, s_gsh, s_gex, s_tsh, s_tex = (sem(n) for n in (
            "h2_written", "group_logits_shifted", "group_exp_ready", "top_logits_shifted", "top_exp_ready"))
        s_rr, s_sel, s_pos, s_scat, s_idx, s_none, s_clear = (sem(n) for n in (
            "routed_ready", "slot_factors_ready", "positions_ready", "table_written", "indices_ready", "sentinel_made", "table_cleared"))
        s_wr = sem("router_ready")
        s_otab, s_oidx = sem("later_table_read"), sem("later_indices_ready")
        s_lst, s_icg, s_icy = sem("blocks_listed"), sem("gather_index_ready"), sem("scatter_index_ready")
        s_xt, s_xgT, s_gu, s_gusb, s_guT, s_sg, s_hE, s_dn, s_ysb = (sem(n) for n in (
            "tokens_transposed", "tokensT_ready", "gate_up_in_psum", "gate_up_copied", "gate_up_transposed",
            "silu_ready", "hidden_ready", "down_in_psum", "expert_rows_ready"))
        s_xg, s_yst = ([sem(f"{n}{i}") for i in range(NB)] for n in ("tokens_gathered", "expert_rows_scattered"))
        s_yl = [sem(f"expert_rows_loaded{i}") for i in range(3)]
        s_zero, s_x3, s_fin = sem("gather_buffer_zeroed"), sem("residual_added"), sem("final_rows_ready")

        w_in = t["w_in"][0]
        cache = {"K": t["cache_k"][0].rearrange("g r h d -> g r (h d)"), "V": t["cache_v"][0].rearrange("g r h d -> g r (h d)")}
        y_rows = ys.rearrange("(t c q) n -> t c (q n)", c=2, q=4)
        h_rows = hs.rearrange("(t q) n -> t (q n)", q=4)
        ident8 = ident[0:NS, 0:NS]
        ones = L["ones"]
        BLOCKS = ((2, NS), (0, P), (1, P))

        def count_full(*label):
            b, n = turn[label]
            return filled[b], n + 1

        def count_taken(*label):
            b, n = turn[label]
            return taken[b], n + 1

        last_use = {("w", c): ("proj", c, 1) for c in range(4)}
        last_use.update({("g", n): ("gate", GPS * n + GPS - 1) for n in range(4)})
        last_use.update({("V", b): ("dpv", b) for b in range(NS)})
        last_use.update({("up", 0): ("up", DK - 1), ("up", 1): ("merge", DK - 1), ("out", 0): ("out", 2 * PB - 1), ("out", 1): ("out", 2 * PB - 1)})

        def count_used(item):
            return (s_kused, 4 * item[1] + 4) if item[0] == "K" else count_full(*last_use[item])

        def wait_loaded(eng, *item):
            eng.wait_ge(s_slot[where[item]], loaded[item])
            return slot[where[item]]

        def load_matrix(eng, e, m, q):
            src = t[("w_gate", "w_up", "w_down")[m]][0, bass.ds(e, 1)]
            if m < 2:
                eng.dma_start(slot[q], src.rearrange("e (p k) f -> p (e k f)", p=P)).then_inc(s_slot[q], 16)
            else:
                eng.dma_start(slot[q].rearrange("p (j n) -> p j n", j=FC), src.rearrange("e (j p) n -> p (e j) n", p=P)).then_inc(s_slot[q], 16)

        FIRST = len(range(0, EXPERTS, NB))
        AFTER = [SLOT_BASE[m] + 16 * FIRST for m in range(3)]
        by_block = table.rearrange("(j s e) c -> j s e c", s=CAP, e=EXPERTS)

        def later_blocks(eng, step, before=lambda: None):
            eng.wait_ge(*count_taken("blocks"))
            count = eng.value_load(blkI[0:1, 0:1], min_val=0, max_val=MAXOVER)
            with eng.If(count > 0):
                before()
                with eng.Fori(0, count) as r:
                    step(r)
            return count

        block = ctx.enter_context(nc.Block())

        @block.sync
        def _(sp):
            sp.dma_start(x[0:NS, 2, :], t["x_sample"].rearrange("b s d -> (b s) d")).then_inc(in_xs, 16)
            sp.dma_start(cea[:], t["c_early"]).then_inc(in_ce, 16)
            sp.dma_start(x[:, 0:PB, :], t["x_prompt"][0].rearrange("(b p) d -> p b d", p=P)).then_inc(in_xp, 16)
            for item in STREAM:
                for last in before[item]:
                    sp.wait_ge(*count_used(last))
                kind, a = item
                dst, done = slot[where[item]], s_slot[where[item]]
                if kind in "wg":
                    first = a * DC if kind == "w" else W_GATE + a * DC
                    sp.dma_start(dst.rearrange("p (k n) -> p k n", k=DK),
                                 w_in[:, first:first + DC].rearrange("(p k) n -> p k n", p=P)).then_inc(done, 16)
                elif kind in "KV":
                    if item == ("K", 0):
                        sp.wait_ge(in_ptab, 16)
                    for j in range(PAGES):
                        page = sp.value_load(ptab[0:1, a * PAGES + j:a * PAGES + j + 1], min_val=0, max_val=NPHYS - 1)
                        sp.dma_start(dst[:, j * DC:(j + 1) * DC],
                                     cache[kind][bass.ds(page, 1)].rearrange("g r n -> (g r) n")).then_inc(done, 16)
                else:
                    src = (t["w_up_pool"][0] if a == 0 else t["w_up_att"][0]) if kind == "up" else t["w_out"][0, a * DC:(a + 1) * DC]
                    sp.dma_start(dst.rearrange("p (k n) -> p k n", k=CC), src.rearrange("(k p) n -> p k n", p=P)).then_inc(done, 16)
            for q in FREED:
                if q < FRONT:
                    sp.wait_ge(*count_used([i for i in STREAM if where[i] == q][-1]))
                elif q == 6:
                    sp.wait_ge(*count_full("pv", HEADS - 1))
                    sp.wait_ge(*count_full("pool", CC - 1))
                    sp.wait_ge(out_tok, 16 * 3)
                elif q == 7:
                    sp.wait_ge(*count_full("merge", DK - 1))
                else:
                    sp.wait_ge(s_hs, 16 * 2)
                    for i in range(len(TPOSE)):
                        sp.wait_ge(*count_full("hT", 1, i))
                load_matrix(sp, q // 3, q % 3, q)
            with sp.Fori(0, (EXPERTS - 5) // 3) as i:
                for r in range(3):
                    sp.wait_ge(s_gu, 3 * i + r + 1)
                    load_matrix(sp, 3 * i + (3 + r), 0, 3 * r)
                    load_matrix(sp, 3 * i + (3 + r), 1, 3 * r + 1)
                    sp.wait_ge(s_dn, 3 * i + r + 1)
                    load_matrix(sp, 3 * i + (3 + r), 2, 3 * r + 2)
            for e in range(EXPERTS - 2, EXPERTS):
                sp.wait_ge(s_gu, e - 2)
                load_matrix(sp, e, 0, 3 * (e % 3))
                load_matrix(sp, e, 1, 3 * (e % 3) + 1)
                sp.wait_ge(s_dn, e - 2)
                load_matrix(sp, e, 2, 3 * (e % 3) + 2)

            def later_block(r):
                sp.wait_ge(s_dn, r + EXPERTS)
                e = sp.value_load(blkI[0:1, bass.ds(r + 1, 1)], min_val=0, max_val=EXPERTS - 1)
                for mat in range(3):
                    load_matrix(sp, e, mat, mat)
                j = sp.value_load(blkI[0:1, bass.ds(r + (1 + MAXOVER), 1)], min_val=0, max_val=7)
                for q in range(4):
                    sp.dma_start(otab[CAP * q:CAP * (q + 1)], by_block[bass.ds(j + 1, 1), :, bass.ds(e, 1)].rearrange("j s e c -> (j s) (e c)")).then_inc(s_otab, 16)
            n_later = later_blocks(sp, later_block, lambda: sp.wait_ge(s_scat, 16 * 6))
            sp.wait_ge(s_yst[0], 16 * n_later + 16 * FIRST)
            for p in range(1, NB):
                sp.wait_ge(s_yst[p], 16 * len(range(p, EXPERTS, NB)))
            sp.dma_start(yload[0:NS, 2], y_rows[SEQ:TOK]).then_inc(s_yl[0], 16)
            sp.dma_start(yload[:, 0], y_rows[0:P]).then_inc(s_yl[1], 16)
            sp.dma_start(yload[:, 1], y_rows[P:2 * P]).then_inc(s_yl[2], 16)
            y_out = t["y_prompt"][0].rearrange("(b p) d -> p b d", p=P)
            for b in range(PB):
                sp.wait_ge(s_fin, b + 1)
                sp.dma_start(y_out[:, b], x[:, b, :]).then_inc(out_y, 16)
            sp.wait_ge(s_fin, PB + 1)
            sp.dma_start(t["y_sample"].rearrange("b s d -> (b s) d"), x[0:NS, 2, :]).then_inc(out_y, 16)
            sp.wait_ge(out_y, 16 * 3)
            sp.wait_ge(out_tok, 16 * 3)
            sp.wait_ge(out_pool, 16 * 6)

        @block.gpsimd
        def _(pool):
            g = nc.gpsimd
            g.memset(none, NONE).then_inc(s_none, 1)
            pool.wait_ge(s_none, 1)
            g.dma_start(table.rearrange("(p n) c -> p (n c)", p=P), none).then_inc(s_clear, 16)
            g.dma_start(t["new_pool_sample"][0, :, 0:PLEN - 1, :], t["state_pool"][0, :, 1:PLEN, :]).then_inc(out_pool, 16)
            pool.wait_ge(in_pidx, 16)
            g.indirect_dma_start(lfp[0:NS * PAGES, :], None, t["cache_logf"][0].rearrange("g r h -> g (r h)"),
                                 bass.IndirectOffsetOnAxis(pidx[:, 0:1], 0), bounds_check=NPHYS - 1).then_inc(in_lfp, 16)
            pool.wait_ge(in_route, 16 * 6)
            g.tensor_copy(wr[:, :, 0:EXPERTS].rearrange("p k (g e) -> p k g e", g=GROUPS), wre[:].rearrange("p g (k e) -> p k g e", k=DK)).then_inc(s_wr, 1)
            g.tensor_copy(wr[:, :, EXPERTS:], wrg[:].rearrange("p (k g) -> p k g", k=DK)).then_inc(s_wr, 1)
            for step, a in PLAN:
                if step == "dq":
                    pool.wait_ge(s_qd, 16)
                    if a >= 2:
                        pool.wait_ge(s_kprod, 4 * (a - 1))
                    g.dma_start(qb[:, a % 2], qd[a].partition_broadcast(P)).then_inc(s_qb[a % 2], 16)
                elif step == "forgetT":
                    pool.wait_ge(*count_taken("forgetT"))
                    g.dma_start(t["new_logf_prompt"][0, 0].rearrange("(b p) n -> p b n", p=P), lft[:, 0:2]).then_inc(out_pool, 16)
                    g.dma_start(t["new_logf_sample"][0, :, 0], lft[0:NS, 2]).then_inc(out_pool, 16)
                elif step == "proj" and a != C_Q:
                    for b in range(PB):
                        pool.wait_ge(*count_taken("proj", a, b))
                    pool.wait_ge(*count_taken("sum", a))
                    if a == C_U:
                        g.dma_start(t["new_pool_prompt"][0, 0], tok[P - PLEN:P, 1, C_U, :]).then_inc(out_tok, 16)
                        g.dma_start(t["new_pool_sample"][0, :, PLEN - 1, :], samp[0:NS, C_U, :]).then_inc(out_pool, 16)
                    else:
                        k = "k" if a == C_K else "v"
                        g.dma_start(t[f"new_{k}_prompt"][0, 0].rearrange("(b p) h d -> p b (h d)", p=P), tok[:, :, a, :]).then_inc(out_tok, 16)
                        g.dma_start(t[f"new_{k}_sample"][0, :, 0].rearrange("b h d -> b (h d)"), samp[0:NS, a, :]).then_inc(out_pool, 16)
            pool.wait_ge(s_zero, 1)
            pool.wait_ge(s_hs, 16 * 2)
            pool.wait_ge(s_idx, 1)
            nought = pool.alloc_register("nought")
            pool.reg_mov(nought, 0)
            g.memset(zeroI, 0).then_inc(s_none, 1)
            pool.wait_ge(s_none, 2)
            h_last, y_last = pool.alloc_register("last_h_row"), pool.alloc_register("last_y_row")

            def gather(n, p, rows):
                g.tensor_tensor(icolg[:, p:p + 1], rows, zeroI, ALU.add).then_inc(s_icg, 1)
                pool.wait_ge(s_icg, n + 1)
                pool.reg_add(h_last, nought, TOK * 4 - 1)
                g.indirect_dma_start(xg[:, p], None, hs, bass.IndirectOffsetOnAxis(icolg[:, p:p + 1], 0),
                                     bounds_check=h_last, oob_is_err=False).then_inc(s_xg[p], 16)

            def scatter(n, p, rows):
                pool.wait_ge(s_ysb, n + 1)
                g.tensor_tensor(icoly[:, p:p + 1], rows, zeroI, ALU.add).then_inc(s_icy, 1)
                pool.wait_ge(s_icy, n + 1)
                pool.reg_add(y_last, nought, TOK * 8 - 1)
                g.indirect_dma_start(ys, bass.IndirectOffsetOnAxis(icoly[:, p:p + 1], 0), ysb[:, p], None,
                                     bounds_check=y_last, oob_is_err=False).then_inc(s_yst[p], 16)

            for p in range(NB):
                gather(p, p, gidx[:, 0, p:p + 1])
            with pool.Fori(0, EXPERTS // NB - 1) as i:
                for p in range(NB):
                    pool.wait_ge(s_xt, NB * i + p + 1)
                    gather(NB * i + (p + NB), p, gidx[:, 0, bass.ds(NB * i + (p + NB), 1)])
                    scatter(NB * i + p, p, gidx[:, 1, bass.ds(NB * i + p, 1)])
            for e in range((EXPERTS // NB - 1) * NB, EXPERTS):
                if e + NB < EXPERTS:
                    pool.wait_ge(s_xt, e + 1)
                    gather(e + NB, e % NB, gidx[:, 0, e + NB:e + NB + 1])
                scatter(e, e % NB, gidx[:, 1, e:e + 1])

            def later_block(r):
                pool.wait_ge(s_oidx, r + 1)
                gather(r + EXPERTS, 0, oidx[:, 0:1])
                scatter(r + EXPERTS, 0, oidx[:, 1:2])

            def scatter_table():
                pool.wait_ge(s_clear, 16)
                pool.wait_ge(s_pos, 1)
                for b in range(3):
                    n = NS if b == 2 else P
                    for c in range(2):
                        g.indirect_dma_start(table, bass.IndirectOffsetOnAxis(posI[0:n, b, c:c + 1], 0),
                                             pay[0:n, 4 * b + 2 * c:4 * b + 2 * c + 2], None, bounds_check=RANKS * EXPERTS - 1).then_inc(s_scat, 16)
            later_blocks(pool, later_block, scatter_table)

        @block.scalar
        def _(act):
            s = nc.scalar
            act.dma_start(nmix[:], t["norm_mix"][0].rearrange("(p k) -> p k", p=P)).then_inc(in_nm, 16)
            act.dma_start(pidx[:], t["page_table"].rearrange("b (j o) -> (b j) o", o=1)).then_inc(in_pidx, 16)
            act.dma_start(ptab[:], t["page_table"].rearrange("(o b) j -> o (b j)", o=1)).then_inc(in_ptab, 16)
            act.dma_start(wf[:], w_in[:, W_FORGET:W_FORGET + HEADS].rearrange("(p k) n -> p k n", p=P)).then_inc(in_wf, 16)
            act.dma_start(bf[:], t["b_forget"].rearrange("o n -> n o")).then_inc(in_wf, 16)

            def full(*label):
                act.wait_ge(*count_full(*label))
                return bank[turn[label][0]]

            links = [0]

            def link(ins):
                links[0] += 1
                ins.then_inc(l_act, 1)
                act.wait_ge(l_act, links[0])

            squared = [0]

            def mean_square(b, n, out):
                if squared[0]:
                    act.wait_ge(s_sq, squared[0])
                squared[0] += 1
                s.activation(out[0:n, :], x[0:n, b, :], ACT.Square, scale=D ** -0.5, accum_out=rowsq[0:n, b]).then_inc(s_sq, 1)

            act.wait_ge(s_pad, 4)
            for b, n in BLOCKS:
                act.wait_ge(*((in_xs, 16) if b == 2 else (in_xp, 16)))
                mean_square(b, n, sqout)
            act.dma_start(cla[:], t["c_late"]).then_inc(in_cl, 16)
            act.dma_start(nffn[:], t["norm_ffn"][0].rearrange("(p k) -> p k", p=P)).then_inc(in_route, 16)
            act.dma_start(wre[:], t["w_router_expert"][0].rearrange("g (p k) e -> p g (k e)", p=P)).then_inc(in_route, 16)
            act.dma_start(wrg[:], t["w_router_group"][0].rearrange("(p k) g -> p (k g)", p=P)).then_inc(in_route, 16)
            act.dma_start(br[0:EXPERTS], t["b_router_expert"][0].rearrange("g (e o) -> (g e) o", o=1)).then_inc(in_route, 16)
            act.dma_start(br[EXPERTS:EXPERTS + GROUPS], t["b_router_group"].rearrange("o n -> n o")).then_inc(in_route, 16)
            act.dma_start(pay[:], t["c_pay"]).then_inc(in_route, 16)
            for i in range(len(TPOSE)):
                act.wait_ge(*count_full("hT", 0, i))
            act.dma_start(cpa[:], t["c_pool"]).then_inc(in_pool, 16)
            act.dma_start(state[0:NS * PLEN, :], t["state_pool"][0].rearrange("b j n -> (b j) n")).then_inc(in_pool, 16)
            act.dma_start(wpool[:], t["w_pool"][0].rearrange("g p n -> p g n")).then_inc(in_pool, 16)
            act.dma_start(pscale[:], t["pool_scale"][0].rearrange("(g p) -> p g", p=P), allow_slow_non_contiguous=True).then_inc(in_pool, 16)

            for step, a in PLAN:
                if step == "proj":
                    src = full("part", a)
                    if a == C_Q:
                        act.wait_ge(s_clear, 16)
                    if turn["sum", a][1]:
                        act.wait_ge(filled[SUM], turn["sum", a][1])
                    s.copy(part[:], src[:]).then_inc(taken[PART], 1)
                    for b in range(PB):
                        src = full("proj", a, b)
                        s.copy(tok[:, b, a, :], src[:]).then_inc(taken[turn["proj", a, b][0]], 1)
                    if a == C_Q:
                        act.wait_ge(*count_taken("sum", C_Q))
                        s.activation(qs, samp[0:NS, C_Q], ACT.Copy, scale=QSCALE).then_inc(s_qs, 1)
                        act.wait_ge(s_qs, 1)
                        act.dma_start(qd, qs).then_inc(s_qd, 16)
                elif step == "forget":
                    act.wait_ge(s_fz, 1)
                    link(s.activation(f_e, f_z, ACT.Abs))
                    s.activation(f_e, f_e, ACT.Exp, scale=-1.0).then_inc(s_fexp, 1)
                    act.wait_ge(s_fw, 1)
                    s.activation(f_ln, f_w, ACT.Ln).then_inc(s_fln, 1)
                elif step == "pages":
                    s.copy(lfT, full("pagesT")[:]).then_inc(taken[SCORES], 1)
                elif step == "bias":
                    s.copy(biasd, full("bias")[:]).then_inc(taken[SCORES], 1)
                elif step == "qk":
                    out = (qT, kT)[a // 2][:, :, (a % 2) * P:(a % 2 + 1) * P]
                    src = full("qk", a)[:].rearrange("p (c n) -> p c n", c=CC)
                    s.activation(out, src, ACT.Copy, scale=QSCALE if a < 2 else 1.0).then_inc(taken[turn["qk", a][0]], 1)
                elif step == "dshift":
                    act.wait_ge(*count_taken("dshift", a))
                    if a:
                        act.wait_ge(*count_full("den", a - 1))
                    else:
                        act.wait_ge(s_pad, 3)
                    s.activation(pex[:, :, 0:HEADS], scs[:, a % 2], ACT.Exp).then_inc(s_pex, 1)
                elif step == "pool":
                    if a < CC:
                        src = full("pool", a)
                        if a >= 2:
                            act.wait_ge(*count_full("mix", a - 2))
                        s.copy(pooledT[:, a % 2], src[:, 0:TOK]).then_inc(taken[turn["pool", a][0]], 1)
                    if a:
                        src = full("mix", a - 1)
                        if a == 1:
                            act.wait_ge(in_pool, 16 * 4)
                        s.activation(mixedT[:, a - 1], src[:, 0:TOK], ACT.Copy, scale=pscale[:, a - 1:a]).then_inc(taken[turn["mix", a - 1][0]], 1)
                elif step == "gate":
                    src = full("gate", a)
                    s.activation(gates[:, a], src[:, 0:TOK], ACT.Tanh, scale=0.5).then_inc(taken[turn["gate", a][0]], 1)
                elif step == "head":
                    if a:
                        src = full("pT", a - 1)
                        if a >= 2:
                            act.wait_ge(*count_full("pv", a - 2))
                        s.copy(probsT, src[:, 0:3 * P]).then_inc(taken[TR], 1)
                    if a < HEADS:
                        act.wait_ge(s_rmax, a + 1)
                        pr = probs[:, a % 2]
                        s.activation(pr[:, 0:P], pr[:, 0:P], ACT.Exp, bias=hmax[:, 0:1], accum_out=hsum[:, 0:1]).then_inc(s_exp, 1)
                        s.activation(pr[:, P:3 * P], pr[:, P:3 * P], ACT.Exp, bias=hmax[:, 1:2], accum_out=hsum[:, 1:2]).then_inc(s_exp, 1)
                elif step == "out":
                    for half in range(2):
                        src = full("opart", half)
                        act.wait_ge(filled[SUM], turn["osum", half][1])
                        s.copy(part[:], src[:]).then_inc(taken[turn["opart", half][0]], 1)
                elif step == "norm":
                    act.wait_ge(s_pad, 5)
                    for i, (b, n) in enumerate(BLOCKS):
                        if b == 2:
                            act.wait_ge(*count_taken("osum", 1))
                            act.wait_ge(*count_full("up", DK - 1))
                        else:
                            act.wait_ge(*count_taken("out", 2 * b))
                            act.wait_ge(*count_taken("out", 2 * b + 1))
                        mean_square(b, n, sqout)
                    act.wait_ge(s_h, 4)
                    act.dma_start(h_rows[SEQ:TOK], h[0:NS, 2]).then_inc(s_hs, 16)
                    act.wait_ge(s_h, 6)
                    act.dma_start(h_rows[0:SEQ].rearrange("(b p) n -> p b n", p=P), h[:, 0:PB]).then_inc(s_hs, 16)
                elif step == "route":
                    act.wait_ge(out_pool, 16 * 6)
                    act.dma_start(normf[:], t["norm_final"].partition_broadcast(P)).then_inc(in_nf, 16)
                    act.wait_ge(s_gsh, 1)
                    s.activation(gex, gex, ACT.Exp).then_inc(s_gex, 1)
                    act.wait_ge(s_tsh, 1)
                    s.activation(tex, tex, ACT.Exp).then_inc(s_tex, 1)

            def hidden(n):
                act.wait_ge(s_guT, n + 1)
                s.activation(sg, bank[QB][:, 0:256].rearrange("p (c g s) -> p c g s", c=2, g=4)[:, :, 0:2], ACT.Silu).then_inc(s_sg, 1)

            with act.Fori(0, EXPERTS) as e:
                hidden(e)
            later_blocks(act, lambda r: hidden(r + EXPERTS))
            act.wait_ge(s_pad, 6)
            for i, (b, n) in enumerate(BLOCKS):
                act.wait_ge(s_x3, i + 1)
                mean_square(b, n, sqend)

        @block.vector
        def _(dve):
            v = nc.vector
            links = [0]

            def link(ins):
                links[0] += 1
                ins.then_inc(l_dve, 1)
                dve.wait_ge(l_dve, links[0])

            def full(*label):
                dve.wait_ge(*count_full(*label))
                return bank[turn[label][0]]

            v.memset(hT[:, :, TOK:TPAD], 0.0).then_inc(s_pad, 1)
            v.memset(pex, 0.0).then_inc(s_pad, 1)
            link(v.memset(psm, 1.0))
            v.memset(snew, -BIG).then_inc(s_pad, 1)
            v.memset(rowsq[:], 1.0).then_inc(s_pad, 1)

            def roots(blocks, n):
                a, r, t2 = rowsq[0:n, blocks], root[0:n, blocks], rowt[0:n, blocks]
                link(v.tensor_scalar(a, a, EPS, None, ALU.add))
                link(v.tensor_scalar(r.bitcast(I32), a.bitcast(I32), 1, None, ALU.logical_shift_right))
                link(v.tensor_scalar(r.bitcast(I32), r.bitcast(I32), -1.0, float(0x5f3759df), ALU.mult, ALU.add))
                link(v.tensor_scalar(a, a, -0.5, None, ALU.mult))
                for _ in range(3):
                    link(v.tensor_tensor(t2, r, r, ALU.mult))
                    link(v.tensor_tensor(t2, t2, a, ALU.mult))
                    link(v.scalar_tensor_tensor(r, t2, 1.5, r, ALU.add, ALU.mult))

            def normalise(b, n):
                v.tensor_scalar(h[0:n, b].rearrange("t (k p) -> t p k", k=DK), x[0:n, b].rearrange("t (p k) -> t p k", k=DK), root[0:n, b], None,
                                ALU.mult).then_inc(s_h, 1)

            def transposed(which, norm, banks):
                for i in banks:
                    k, b, half = TPOSE[i]
                    src = full("hT", which, i)
                    if b == 2:
                        v.tensor_tensor(hT[:, :, SEQ:TOK], src[:, 0:DK * NS].rearrange("p (k t) -> p k t", k=DK),
                                        norm[:].unsqueeze(2).to_broadcast([P, DK, NS]), ALU.mult).then_inc(taken[k], 1)
                    else:
                        ks = slice(4 * half, 4 * half + 4)
                        v.tensor_tensor(hT[:, ks, b * P:(b + 1) * P], src[:].rearrange("p (k t) -> p k t", k=4),
                                        norm[:, ks].unsqueeze(2).to_broadcast([P, 4, P]), ALU.mult).then_inc(taken[k], 1)

            dve.wait_ge(s_sq, 3)
            roots(slice(0, 3), P)
            v.memset(rowsq[:], 1.0).then_inc(s_pad, 1)
            for b, n in BLOCKS:
                normalise(b, n)
            dve.wait_ge(in_nm, 16)
            transposed(0, nmix, range(5))

            def add_out(i):
                xs = x[:, i // 2, (i % 2) * 512:(i % 2 + 1) * 512]
                v.scalar_tensor_tensor(xs, full("out", i)[:], 0.5, xs, ALU.mult, ALU.add).then_inc(taken[turn["out", i][0]], 1)

            def run_plan():
                for step, a in PLAN:
                    if step == "proj":
                        v.tensor_copy(samp[0:NS, a, :], full("sum", a)[0:NS, :]).then_inc(taken[SUM], 1)
                    elif step == "forget":
                        dve.wait_ge(in_wf, 32)
                        v.tensor_scalar(f_z, full("forget")[0:HEADS, 0:TOK], bf[:, 0:1], None, ALU.add).then_inc(s_fz, 1)
                        dve.wait_ge(s_fz, 1)
                        v.tensor_scalar(f_min, f_z, 0.0, None, ALU.min).then_inc(taken[CHAIN], 1)
                        dve.wait_ge(s_fexp, 1)
                        v.tensor_scalar(f_w, f_e, 1.0, None, ALU.add).then_inc(s_fw, 1)
                        dve.wait_ge(s_fw, 1)
                        link(v.tensor_scalar(f_z, f_w, 1.0, None, ALU.subtract))
                        dve.wait_ge(s_fln, 1)
                        link(v.tensor_tensor(f_ln, f_ln, f_e, ALU.mult))
                        link(v.tensor_scalar(f_w, f_z, 1e-30, None, ALU.max))
                        link(v.reciprocal(f_w, f_w))
                        link(v.tensor_tensor(f_ln, f_ln, f_w, ALU.mult))
                        link(v.tensor_scalar(f_z, f_z, 0.0, None, ALU.is_equal))
                        link(v.tensor_tensor(f_z, f_z, f_e, ALU.mult))
                        link(v.tensor_tensor(f_ln, f_ln, f_z, ALU.add))
                        link(v.tensor_tensor(lf8, f_min, f_ln, ALU.subtract))
                        link(v.memset(f_w, 1.0))
                        link(v.tensor_tensor_scan(f_e[:, 0:SEQ], f_w[:, 0:SEQ], lf8[:, 0:SEQ], 0.0, ALU.mult, ALU.add))
                        v.tensor_scalar(cneg, f_e[:, 0:SEQ], -1.0, None, ALU.mult).then_inc(s_lf, 1)
                    elif step == "forgetT":
                        src = full("forgetT")
                        link(v.tensor_scalar(cq, src[:, 0:16].rearrange("p (b n) -> p b n", b=2), -1.0, None, ALU.mult))
                        link(v.tensor_copy(lft[:, 0:2], src[:, 16:32].rearrange("p (b n) -> p b n", b=2)))
                        v.tensor_copy(lft[0:NS, 2], src[0:NS, 32:40]).then_inc(taken[CHAIN], 1)
                    elif step == "pages":
                        dve.wait_ge(in_cl, 16)
                        dve.wait_ge(*count_taken("sum", C_V))
                        dve.wait_ge(s_pad, 3)
                        dve.wait_ge(s_qd, 16)
                        link(v.tensor_tensor(mk[0:NS], samp[0:NS, C_Q, :], samp[0:NS, C_K, :], ALU.mult))
                        link(v.tensor_reduce(dsc[0:NS, 0:HEADS], mk[0:NS].rearrange("p (h d) -> p h d", h=HEADS), AX.X, ALU.add))
                        link(v.tensor_scalar(dsc[0:NS, 0:HEADS], dsc[0:NS, 0:HEADS], QSCALE, None, ALU.mult))
                        link(v.tensor_tensor(snew[0:NS], dsc[0:NS, 0:HEADS].unsqueeze(1).to_broadcast([NS, NS, HEADS]),
                                        L["other"][0:NS].unsqueeze(2).to_broadcast([NS, NS, HEADS]), ALU.add))
                        dve.wait_ge(*count_taken("pagesT"))
                        lt = lfT.rearrange("p (m j) -> p m j", j=PAGES)
                        lc = lfC.rearrange("p (m j) -> p m j", j=PAGES)
                        link(v.memset(lc[:, :, PAGES - 1], 0.0))
                        for j in range(PAGES - 2, -1, -1):
                            link(v.tensor_tensor(lc[:, :, j], lc[:, :, j + 1], lt[:, :, j + 1], ALU.add))
                        dve.wait_ge(*count_taken("forgetT"))
                        v.tensor_tensor(lfd.rearrange("p (h b j) -> p h b j", h=HEADS, b=NS)[0:NS],
                                        lft[0:NS, 2].unsqueeze(2).unsqueeze(3).to_broadcast([NS, HEADS, NS, PAGES]),
                                        ident8.unsqueeze(1).unsqueeze(3).to_broadcast([NS, HEADS, NS, PAGES]), ALU.mult).then_inc(s_lfd, 1)
                    elif step[:4] == "keys":
                        pair, sc = int(step[4:]), scs[:, a % 2]
                        ks = wait_loaded(dve, "K", a).rearrange("p (j n) -> p j n", j=PAGES)[:, 2 * pair:2 * pair + 2]
                        dve.wait_ge(s_qb[a % 2], 16 * (a // 2) + 16)
                        v.tensor_tensor(ks, ks, qb[:, a % 2].unsqueeze(1).to_broadcast([P, 2, DC]), ALU.mult).then_inc(s_kprod, 1)
                        dve.wait_ge(s_kprod, 4 * a + pair + 1)
                        if a >= 2:
                            dve.wait_ge(s_pex, a - 1)
                        v.tensor_reduce(sc[:, 2 * pair:2 * pair + 2], ks.rearrange("p j (h d) -> p j h d", h=HEADS), AX.X, ALU.add).then_inc(s_kused, 1)
                        if pair == PAGES // 2 - 1:
                            dve.wait_ge(s_kused, 4 * a + 4)
                            if a == 0:
                                dve.wait_ge(*count_taken("bias"))
                            bias = biasd.rearrange("p (h b j) -> p b j h", h=HEADS, b=NS)[:, a]
                            link(v.tensor_tensor(sc[:, 0:PAGES], sc[:, 0:PAGES], bias, ALU.add))
                            link(v.tensor_copy(sc[:, PAGES], snew[:, a]))
                            v.tensor_reduce(m1, sc.rearrange("p j h -> p h j"), AX.X, ALU.max).then_inc(s_m1, 1)
                    elif step == "dmax":
                        link(v.tensor_reduce(nmax, full("dmax", a)[0:HEADS, 0:P], AX.X, ALU.max, negate=True))
                        v.tensor_scalar(dg, ident8, nmax, None, ALU.mult).then_inc(taken[CHAIN], 1)
                    elif step == "dshift":
                        sc = scs[:, a % 2]
                        v.tensor_tensor(sc, sc, full("dshift", a)[:, 0:HEADS].unsqueeze(1).to_broadcast([P, PAGES + 1, HEADS]), ALU.add).then_inc(taken[CHAIN], 1)
                    elif step == "dsums":
                        dve.wait_ge(s_pex, a + 1)
                        v.tensor_reduce(psm.rearrange("p (g h) -> p g h", g=4)[:, :, 0:HEADS], pex[:, :, 0:HEADS].rearrange("p j h -> p h j").unsqueeze(1).to_broadcast([P, 4, HEADS, PAGES + 1]), AX.X, ALU.add).then_inc(s_psm, 1)
                    elif step == "dpv":
                        v.reciprocal(rden, full("den", a)[:, 0:1]).then_inc(taken[CHAIN], 1)
                    elif step == "dsum":
                        dve.wait_ge(*count_taken("den", a))
                        if a:
                            dve.wait_ge(*count_full("datt", a - 1))
                        v.scalar_tensor_tensor(mk.rearrange("p (h d) -> p h d", h=HEADS),
                                               full("dpv", a)[:].rearrange("p (h d) -> p h d", h=HEADS), rden,
                                               L["own"].unsqueeze(2).to_broadcast([P, HEADS, HD]), ALU.mult, ALU.mult).then_inc(taken[PART], 1)
                    elif step == "datt":
                        v.tensor_copy(attT[:, :, SEQ + a], full("datt", a)[:, 0:CC]).then_inc(taken[CHAIN], 1)
                    elif step == "hnorm":
                            pr = probs[:, a % 2]
                            dve.wait_ge(s_exp, 2 * a + 2)
                            link(v.reciprocal(hinv, hsum))
                            v.tensor_scalar(pr[:, 0:P], pr[:, 0:P], hinv[:, 0:1], None, ALU.mult)
                            v.tensor_scalar(pr[:, P:3 * P], pr[:, P:3 * P], hinv[:, 1:2], None, ALU.mult).then_inc(s_probs, 1)
                    elif step == "head":
                        if a < HEADS:
                            src, pr = full("scores", a), probs[:, a % 2]
                            if a >= 2:
                                dve.wait_ge(*count_full("pT", a - 2))
                            v.scalar_tensor_tensor(pr[:, 0:P], src[:, 0:P], cq[:, 0, a:a + 1], L["mask"][:, P:2 * P], ALU.add, ALU.add)
                            v.scalar_tensor_tensor(pr[:, P:3 * P], src[:, P:3 * P], cq[:, 1, a:a + 1], L["mask"], ALU.add, ALU.add).then_inc(taken[SCORES], 1)
                            dve.wait_ge(*count_taken("scores", a))
                            v.tensor_reduce(hmax[:, 0:1], pr[:, 0:P], AX.X, ALU.max, negate=True)
                            v.tensor_reduce(hmax[:, 1:2], pr[:, P:3 * P], AX.X, ALU.max, negate=True).then_inc(s_rmax, 1)
                    elif step == "pv":
                        r = HD * (a % 2)
                        v.tensor_copy(attT[r:r + HD, a // 2, 0:SEQ], full("pv", a)[r:r + HD, 0:SEQ]).then_inc(taken[TR], 1)
                    elif step == "up":
                        dve.wait_ge(*count_taken("gate", a))
                        v.scalar_tensor_tensor(gates[:, a], gates[:, a], 1.0, full("up", a)[:, 0:TOK], ALU.add, ALU.mult).then_inc(taken[turn["up", a][0]], 1)
                    elif step == "merge":
                        dve.wait_ge(*count_taken("gate", DK + a))
                        dve.wait_ge(*count_taken("up", a))
                        v.scalar_tensor_tensor(gates[:, DK + a], gates[:, DK + a], 1.0, full("merge", a)[:, 0:TOK], ALU.add, ALU.mult).then_inc(taken[turn["merge", a][0]], 1)
                        dve.wait_ge(*count_taken("merge", a))
                        v.tensor_tensor(hT[:, a, 0:TOK], gates[:, a], gates[:, DK + a], ALU.add).then_inc(s_merge, 1)
                    elif step == "out":
                        for half in range(2):
                            xs = x[0:NS, 2, half * 512:(half + 1) * 512]
                            v.scalar_tensor_tensor(xs, full("osum", half)[0:NS], 0.5, xs, ALU.mult, ALU.add).then_inc(taken[SUM], 1)
                            add_out(half)
                    elif step == "norm":
                        dve.wait_ge(s_sq, 5)
                        dve.wait_ge(s_merge, DK)
                        roots(slice(0, 3, 2), P)
                        normalise(2, NS)
                        normalise(0, P)
                        dve.wait_ge(in_route, 16 * 6)
                        add_out(2)
                        add_out(3)
                        for half in range(2):
                            dve.wait_ge(*count_full("opart", half))
                        for i in range(2 * PB):
                            dve.wait_ge(*count_full("out", i))
                        transposed(1, nffn, range(3))
                        dve.wait_ge(s_sq, 6)
                        roots(slice(1, 2), P)
                        normalise(1, P)
                        transposed(1, nffn, range(3, 5))
                    elif step == "route":
                        route()

            def first_of_equals(out, values, top, n, scratch):
                link(v.tensor_reduce(top, values, AX.X, ALU.max))
                link(v.tensor_tensor(scratch, values, top.to_broadcast([P, 3, n]), ALU.is_equal))
                link(v.tensor_tensor(scratch, scratch, L["first"][:, EXPERTS - n:].unsqueeze(1).to_broadcast([P, 3, n]), ALU.mult))
                link(v.tensor_reduce(r_top, scratch, AX.X, ALU.max))
                link(v.tensor_tensor(out, scratch, r_top.to_broadcast([P, 3, n]), ALU.is_equal))

            def route():
                dve.wait_ge(out_pool, 16 * 6)
                v.memset(xg, 0.0).then_inc(s_zero, 1)
                link(v.memset(lgT[0:36], 0.0))
                v.tensor_scalar(lgT[0:36, 0:TOK], full("logits")[0:36, 0:TOK], br[:, 0:1], None, ALU.add).then_inc(taken[PART], 1)
                v.tensor_copy(lg, full("logitsT")[:, 0:3 * 36].rearrange("p (b n) -> p b n", b=3)).then_inc(taken[SUM], 1)
                dve.wait_ge(*count_taken("logitsT"))
                grp = lg[:, :, EXPERTS:]
                first_of_equals(r_oh, grp, r_gm, GROUPS, r_t4)
                v.tensor_tensor(gex, grp, r_gm.to_broadcast([P, 3, GROUPS]), ALU.subtract).then_inc(s_gsh, 1)
                link(v.tensor_scalar(r_oh, r_oh, BIG, -BIG, ALU.mult, ALU.add))
                link(v.tensor_tensor(em.rearrange("p b (g e) -> p b g e", g=GROUPS), lg[:, :, 0:EXPERTS].rearrange("p b (g e) -> p b g e", g=GROUPS),
                                     r_oh.unsqueeze(3).to_broadcast([P, 3, GROUPS, PER_GROUP]), ALU.add))
                first_of_equals(e1, em, r_m1, EXPERTS, ra)
                link(v.scalar_tensor_tensor(em, e1, -2 * BIG, em, ALU.mult, ALU.add))
                first_of_equals(e2, em, r_m2, EXPERTS, ra)
                link(v.tensor_tensor(rr, e1, e2, ALU.add))
                v.tensor_tensor(rr, rr, L["valid"].unsqueeze(2).to_broadcast([P, 3, EXPERTS]), ALU.mult).then_inc(s_rr, 1)
                v.tensor_tensor(tex, r_m2, r_m1, ALU.subtract).then_inc(s_tsh, 1)
                v.tensor_copy(rb, full("ranks")[:, 0:96].rearrange("p (b n) -> p b n", b=3)).then_inc(taken[BIG0], 1)
                dve.wait_ge(*count_taken("ranks"))
                for c, e in enumerate((e1, e2)):
                    link(v.tensor_tensor(ra, e, rb, ALU.mult))
                    link(v.tensor_reduce(rank[:, :, c], ra, AX.X, ALU.add))
                    for i in range(2):
                        v.tensor_tensor(selE[:, :, c, i], e, L["pay"].rearrange("p (b c i) -> p b c i", b=3, c=2)[:, :, c, i:i + 1].to_broadcast([P, 3, EXPERTS]), ALU.mult)
                v.tensor_tensor(selS, L["slots"].unsqueeze(1).unsqueeze(1).to_broadcast([P, 3, 2, CAP]),
                                rank.unsqueeze(3).to_broadcast([P, 3, 2, CAP]), ALU.is_equal).then_inc(s_sel, 1)
                v.tensor_scalar(gidx[:].rearrange("p i e -> p (i e)"), full("slots")[:, 0:2 * EXPERTS], 4.0, L["group4"], ALU.mult, ALU.add).then_inc(s_idx, 1)
                for c, e in enumerate((e1, e2)):
                    link(v.tensor_tensor(ra, e, L["expert"].unsqueeze(1).to_broadcast([P, 3, EXPERTS]), ALU.mult))
                    link(v.tensor_reduce(slotpos[:, :, c], ra, AX.X, ALU.add))
                v.scalar_tensor_tensor(posI[:], rank, float(EXPERTS), slotpos, ALU.mult, ALU.add).then_inc(s_pos, 1)
                link(v.tensor_tensor(over.rearrange("p (e j) -> p e j", j=8), full("totals")[:, 0:EXPERTS].unsqueeze(2).to_broadcast([P, EXPERTS, 8]),
                                     L["block"].unsqueeze(1).to_broadcast([P, EXPERTS, 8]), ALU.is_gt))
                link(v.memset(ones8, 1.0))
                link(v.tensor_tensor_scan(cs, ones8, over, 0.0, ALU.mult, ALU.add))
                link(v.tensor_scalar(over, cs, L["part"], None, ALU.is_le))
                v.tensor_reduce(lst, over, AX.X, ALU.add).then_inc(s_lst, 1)
                v.tensor_copy(blkI[0:1, 0:1], cs[0:1, 255:256])
                link(v.tensor_copy(blkI[0:1, 1:1 + MAXOVER], full("blocks")[0:1, 0:MAXOVER]))
                link(v.tensor_scalar(blkI[0:1, 1 + MAXOVER:], blkI[0:1, 1:1 + MAXOVER], 7, None, ALU.bitwise_and))
                v.tensor_scalar(blkI[0:1, 1:1 + MAXOVER], blkI[0:1, 1:1 + MAXOVER], 3, None, ALU.logical_shift_right).then_inc(taken[CHAIN], 1)
                dve.wait_ge(s_gex, 1)
                link(v.tensor_reduce(r_gs, gex, AX.X, ALU.add))
                dve.wait_ge(s_tex, 1)
                link(v.tensor_scalar(r_ts, tex, 1.0, None, ALU.add))
                link(v.tensor_tensor(r_gs, r_gs, r_ts, ALU.mult))
                link(v.reciprocal(wts[:, 0].unsqueeze(2), r_gs))
                link(v.tensor_tensor(wts[:, 1].unsqueeze(2), wts[:, 0].unsqueeze(2), tex, ALU.mult))

            run_plan()
            nq = nffn[:].rearrange("p (g c) -> p c g", c=2)

            def block_rows(n, p, used):
                dve.wait_ge(s_xt, n + 1)
                for c in range(2):
                    ins = v.tensor_tensor(xgT[:, c], bank[PART][:, c * P:(c + 1) * P].rearrange("p (g s) -> p g s", g=4),
                                          nq[:, c].unsqueeze(2).to_broadcast([P, 4, CAP]), ALU.mult)
                ins.then_inc(s_xgT, 1)
                dve.wait_ge(s_gu, n + 1)
                v.tensor_copy(gu, bank[SUM][:, 0:256]).then_inc(s_gusb, 1)
                dve.wait_ge(s_sg, n + 1)
                v.tensor_tensor(hE, sg, bank[QB][:, 0:256].rearrange("p (c g s) -> p c g s", c=2, g=4)[:, :, 2:4], ALU.mult).then_inc(s_hE, 1)
                dve.wait_ge(s_dn, n + 1)
                if used is not None:
                    dve.wait_ge(s_yst[p], 16 * used)
                v.tensor_copy(ysb[:, p], bank[CHAIN][:, 0:256]).then_inc(s_ysb, 1)

            def later_block(r):
                dve.wait_ge(s_otab, 64 * (r + 1))
                dve.wait_ge(s_icy, r + EXPERTS)
                v.tensor_scalar(oidx, otab, 4.0, L["group"], ALU.mult, ALU.add).then_inc(s_oidx, 1)
                block_rows(r + EXPERTS, 0, r + FIRST)

            for p in range(NB):
                block_rows(p, p, None)
            with dve.Fori(1, EXPERTS // NB) as i:
                for p in range(NB):
                    block_rows(NB * i + p, p, i)
            for e in range(EXPERTS // NB * NB, EXPERTS):
                block_rows(e, e % NB, e // NB)
            later_blocks(dve, later_block)
            v.memset(rowsq[:], 1.0).then_inc(s_pad, 1)
            for i, (b, n) in enumerate(BLOCKS):
                dve.wait_ge(s_yl[i], 16)
                link(v.scalar_tensor_tensor(x[0:n, b], yload[0:n, b, 0], wts[0:n, 0, b:b + 1], x[0:n, b], ALU.mult, ALU.add))
                v.scalar_tensor_tensor(x[0:n, b], yload[0:n, b, 1], wts[0:n, 1, b:b + 1], x[0:n, b], ALU.mult, ALU.add).then_inc(s_x3, 1)
            dve.wait_ge(in_nf, 16)
            dve.wait_ge(s_sq, 9)
            roots(slice(0, 3), P)
            for b, n in ((0, P), (1, P), (2, NS)):
                v.scalar_tensor_tensor(x[0:n, b], x[0:n, b], root[0:n, b], normf[0:n], ALU.mult, ALU.mult).then_inc(s_fin, 1)

        @block.tensor
        def _(pe):
            m = nc.tensor

            def free(*label):
                b, n = turn[label]
                if n:
                    pe.wait_ge(taken[b], n)
                return bank[b]

            def transposes(which, banks):
                for i in banks:
                    k, b, half = TPOSE[i]
                    out = free("hT", which, i)
                    pe.wait_ge(s_h, 3 * which + (1, 2, 3)[(2, 0, 1).index(b)])
                    if b == 2:
                        for c in range(DK):
                            last = m.transpose(out[:, c * NS:(c + 1) * NS], h[0:NS, 2, c * P:(c + 1) * P], ident8)
                    else:
                        for c in range(4):
                            last = m.transpose(out[:, c * P:(c + 1) * P], h[:, b, (4 * half + c) * P:(4 * half + c + 1) * P], ident)
                    last.then_inc(filled[k], 1)

            pe.wait_ge(in_ce, 16)
            transposes(0, range(3))
            pe.wait_ge(s_pad, 3)

            for step, a in PLAN:
                if step == "proj":
                    w = wait_loaded(pe, "w", a).rearrange("p (k n) -> p k n", k=DK)
                    out = free("part", a)
                    if a == C_Q:
                        pe.wait_ge(*count_taken("hT", 0, 0))
                    for k in range(DK):
                        g = 32 * (k % 4)
                        last = m.matmul(out[g:g + 32, :], hT[:, k, SEQ:TPAD], w[:, k], start=k < 4, stop=k >= 4)
                    last.then_inc(filled[PART], 1)
                    if a == C_Q:
                        transposes(0, range(3, 5))
                    for b in range(PB):
                        out = free("proj", a, b)
                        if a == C_Q:
                            for i in (1 + 2 * b, 2 + 2 * b):
                                pe.wait_ge(*count_taken("hT", 0, i))
                        for k in range(DK):
                            last = m.matmul(out[:], hT[:, k, b * P:(b + 1) * P], w[:, k], start=k == 0, stop=k == DK - 1)
                        last.then_inc(filled[turn["proj", a, b][0]], 1)
                        if b == 0:
                            out = free("sum", a)
                            pe.wait_ge(*count_taken("part", a))
                            m.matmul(out[0:NS, :], E["sum8"], part[:], start=True, stop=True).then_inc(filled[SUM], 1)
                elif step == "forget":
                    out = free("forget")
                    pe.wait_ge(in_wf, 32)
                    for k in range(DK):
                        last = m.matmul(out[0:HEADS, 0:TOK], wf[:, k], hT[:, k, 0:TOK], start=k == 0, stop=k == DK - 1)
                    last.then_inc(filled[CHAIN], 1)
                elif step == "forgetT":
                    out = free("forgetT")
                    pe.wait_ge(s_lf, 1)
                    for b in range(PB):
                        m.transpose(out[:, 8 * b:8 * b + 8], cneg[:, b * P:(b + 1) * P], ident8)
                        m.transpose(out[:, 16 + 8 * b:24 + 8 * b], lf8[:, b * P:(b + 1) * P], ident8)
                    m.transpose(out[0:NS, 32:40], lf8[:, SEQ:TOK], ident8).then_inc(filled[CHAIN], 1)
                elif step == "pages":
                    out = free("pagesT")
                    pe.wait_ge(in_lfp, 16)
                    rows = lfp[0:NS * PAGES].rearrange("p (r h) -> p h r", h=HEADS)
                    for hh in range(HEADS):
                        last = m.transpose(out[:, 64 * hh:64 * hh + 64], rows[:, hh], ident[0:64, 0:64])
                    last.then_inc(filled[SCORES], 1)
                elif step == "bias":
                    out = free("bias")
                    pe.wait_ge(in_cl, 16)
                    pe.wait_ge(s_lfd, 1)
                    m.matmul(out[:], L["later"], lfT, start=True, stop=False)
                    m.matmul(out[:], ones, lfC, start=False, stop=False)
                    m.matmul(out[:], ones[0:NS], lfd[0:NS], start=False, stop=True).then_inc(filled[SCORES], 1)
                elif step == "qk":
                    c0, b = (C_Q, C_K)[a // 2], a % 2
                    out = free("qk", a)
                    pe.wait_ge(*count_taken("proj", c0, b))
                    for c in range(CC):
                        last = m.transpose(out[:, c * P:(c + 1) * P], tok[:, b, c0, c * P:(c + 1) * P], ident)
                    last.then_inc(filled[turn["qk", a][0]], 1)
                elif step == "dmax":
                    out = free("dmax", a)
                    pe.wait_ge(s_m1, a + 1)
                    m.transpose(out[0:HEADS, 0:P], m1, ident).then_inc(filled[CHAIN], 1)
                elif step == "dshift":
                    out = free("dshift", a)
                    m.matmul(out[:, 0:HEADS], ones[0:HEADS], dg, start=True, stop=True).then_inc(filled[CHAIN], 1)
                elif step == "dpv":
                    out = free("dpv", a)
                    pe.wait_ge(s_pex, a + 1)
                    pages = wait_loaded(pe, "V", a).rearrange("p (j n) -> p j n", j=PAGES)
                    for j in range(PAGES):
                        g = 32 * (j % 4)
                        m.matmul(out[g:g + 32, :], pex[:, j], pages[:, j], start=j < 4, stop=j >= 4 and j % 4 > 0)
                    m.matmul(out[0:32, :], pex[0:NS, PAGES], samp[0:NS, C_V], start=False, stop=True).then_inc(filled[PART], 1)
                    out = free("den", a)
                    pe.wait_ge(s_psm, a + 1)
                    m.matmul(out[:, 0:1], psm, ones[:, 0:1], start=True, stop=True).then_inc(filled[CHAIN], 1)
                elif step == "datt":
                    out = free("datt", a)
                    pe.wait_ge(*count_taken("dpv", a))
                    for c in range(CC):
                        last = m.matmul(out[:, c:c + 1], mk[:, c * P:(c + 1) * P], ones[:, 0:1], start=True, stop=True)
                    last.then_inc(filled[CHAIN], 1)
                elif step == "pool":
                    if a < CC:
                        out = free("pool", a)
                        if a == 0:
                            pe.wait_ge(in_pool, 16 * 4)
                            for b in range(PB):
                                pe.wait_ge(*count_taken("proj", C_U, b))
                            pe.wait_ge(*count_taken("sum", C_U))
                        cols = slice(a * P, (a + 1) * P)
                        m.matmul(out[:, 0:P], tok[:, 0, C_U, cols], C["first"][:, a], start=True, stop=True)
                        m.matmul(out[:, P:SEQ], tok[:, 1, C_U, cols], C["full"][:, a], start=True, stop=False)
                        m.matmul(out[:, P:P + PLEN], tok[:, 0, C_U, cols], C["before"][:, a], start=False, stop=True)
                        m.matmul(out[:, SEQ:TOK], state[0:NS * PLEN, cols], C["state"][0:NS * PLEN, a], start=True, stop=False)
                        m.matmul(out[:, SEQ:TOK], samp[0:NS, C_U, cols], C["mine"][0:NS, a], start=False, stop=True).then_inc(filled[turn["pool", a][0]], 1)
                    if a:
                        out = free("mix", a - 1)
                        pe.wait_ge(*count_taken("pool", a - 1))
                        m.matmul(out[:, 0:TOK], wpool[:, a - 1], pooledT[:, (a - 1) % 2], start=True, stop=True).then_inc(filled[turn["mix", a - 1][0]], 1)
                elif step == "gate":
                    w = wait_loaded(pe, "g", a // GPS).rearrange("p (k n) -> p k n", k=DK)
                    out = free("gate", a)
                    cols = slice((a % GPS) * P, (a % GPS + 1) * P)
                    for k in range(DK):
                        last = m.matmul(out[:, 0:TOK], w[:, k, cols], hT[:, k, 0:TOK], start=k == 0, stop=k == DK - 1)
                    last.then_inc(filled[turn["gate", a][0]], 1)
                elif step == "head":
                    if a:
                        out = free("pT", a - 1)
                        pe.wait_ge(s_probs, a)
                        pr = probs[:, (a - 1) % 2]
                        for i in range(3):
                            last = m.transpose(out[:, i * P:(i + 1) * P], pr[:, i * P:(i + 1) * P], ident)
                        last.then_inc(filled[TR], 1)
                    if a < HEADS:
                        out = free("scores", a)
                        if a == 0:
                            for i in range(4):
                                pe.wait_ge(*count_taken("qk", i))
                        r, c = slice(HD * (a % 2), HD * (a % 2) + HD), a // 2
                        onehot = ident8[:, a:a + 1].to_broadcast([NS, P])
                        for b, cols in ((0, slice(0, P)), (1, slice(P, 3 * P))):
                            n = (b + 1) * P
                            m.matmul(out[:, cols], qT[r, c, b * P:(b + 1) * P], kT[r, c, 0:n], start=True, stop=False)
                            last = m.matmul(out[:, cols], onehot, cneg[:, 0:n], start=False, stop=True)
                        last.then_inc(filled[SCORES], 1)
                elif step == "pv":
                    out = free("pv", a)
                    hd = slice(a * HD, (a + 1) * HD)
                    r = slice(HD * (a % 2), HD * (a % 2) + HD)
                    m.matmul(out[r, 0:P], tok[:, 0, C_V, hd], probsT[:, 0:P], start=True, stop=True)
                    m.matmul(out[r, P:SEQ], tok[:, 0, C_V, hd], probsT[:, P:2 * P], start=True, stop=False)
                    m.matmul(out[r, P:SEQ], tok[:, 1, C_V, hd], probsT[:, 2 * P:3 * P], start=False, stop=True).then_inc(filled[TR], 1)
                elif step in ("up", "merge"):
                    w = wait_loaded(pe, "up", int(step == "merge")).rearrange("p (k n) -> p k n", k=CC)
                    out = free(step, a)
                    if a == 0 and step == "up":
                        pe.wait_ge(*count_taken("mix", CC - 1))
                    if a == 0 and step == "merge":
                        pe.wait_ge(*count_taken("datt", NS - 1))
                        pe.wait_ge(*count_taken("pv", HEADS - 1))
                    src = mixedT if step == "up" else attT
                    for k in range(CC):
                        last = m.matmul(out[:, 0:TOK], w[:, k, a * P:(a + 1) * P], src[:, k], start=k == 0, stop=k == CC - 1)
                    last.then_inc(filled[turn[step, a][0]], 1)
                elif step == "out":
                    w = [wait_loaded(pe, "out", i).rearrange("p (k n) -> p k n", k=CC) for i in range(2)]
                    pe.wait_ge(s_merge, DK)
                    for half in range(2):
                        out = free("opart", half)
                        for k in range(DK):
                            g = 32 * (k % 4)
                            last = m.matmul(out[g:g + 32, :], hT[:, k, SEQ:TPAD], w[k // CC][:, k % CC, half * 512:(half + 1) * 512], start=k < 4, stop=k >= 4)
                        last.then_inc(filled[turn["opart", half][0]], 1)
                    for i in range(2 * PB):
                        out = free("out", i)
                        b, half = i // 2, i % 2
                        for k in range(DK):
                            last = m.matmul(out[:], hT[:, k, b * P:(b + 1) * P], w[k // CC][:, k % CC, half * 512:(half + 1) * 512], start=k == 0, stop=k == DK - 1)
                        last.then_inc(filled[turn["out", i][0]], 1)
                        if i < 2:
                            out = free("osum", i)
                            pe.wait_ge(*count_taken("opart", i))
                            m.matmul(out[0:NS, :], E["sum8"], part[:], start=True, stop=True).then_inc(filled[SUM], 1)
                elif step == "norm":
                    transposes(1, range(3))
                    out = free("logits")
                    pe.wait_ge(s_wr, 2)
                    for i in range(3):
                        pe.wait_ge(*count_taken("hT", 1, i))
                    for cols in (slice(0, P), slice(SEQ, TOK)):
                        for k in range(DK):
                            m.matmul(out[0:36, cols], wr[:, k], hT[:, k, cols], start=k == 0, stop=k == DK - 1)
                    transposes(1, range(3, 5))
                    for i in range(3, 5):
                        pe.wait_ge(*count_taken("hT", 1, i))
                    for k in range(DK):
                        last = m.matmul(out[0:36, P:SEQ], wr[:, k], hT[:, k, P:SEQ], start=k == 0, stop=k == DK - 1)
                    last.then_inc(filled[PART], 1)
                elif step == "route":
                    out = free("logitsT")
                    pe.wait_ge(*count_taken("logits"))
                    for b in range(3):
                        last = m.transpose(out[:, 36 * b:36 * b + 36], lgT[0:36, b * P:(b + 1) * P], ident[0:36, 0:36])
                    last.then_inc(filled[SUM], 1)
                    out = free("ranks")
                    pe.wait_ge(s_rr, 1)
                    for b in range(3):
                        for c in range(b + 1):
                            last = m.matmul(out[:, 32 * b:32 * b + 32], L["earlier"] if c == b else ones, rr[:, c], start=c == 0, stop=c == b)
                    last.then_inc(filled[BIG0], 1)
                    out = free("totals")
                    for c in range(3):
                        last = m.matmul(out[:, 0:EXPERTS], ones, rr[:, c], start=c == 0, stop=c == 2)
                    last.then_inc(filled[SCORES], 1)
                    out = free("slots")
                    pe.wait_ge(s_sel, 1)
                    pairs = [(b, c) for b in range(3) for c in range(2)]
                    for q in range(4):
                        for b, c in pairs:
                            last = m.matmul(out[CAP * q:CAP * (q + 1), 0:2 * EXPERTS], selS[:, b, c], selE[:, b, c].rearrange("p i e -> p (i e)"),
                                            start=(b, c) == pairs[0], stop=(b, c) == pairs[-1])
                    last.then_inc(filled[BIG1], 1)
                    out = free("blocks")
                    pe.wait_ge(s_lst, 1)
                    m.matmul(out[0:1, 0:MAXOVER], lst, ident[:, 0:MAXOVER], start=True, stop=True).then_inc(filled[CHAIN], 1)

            def expert(e, p, used, in_slots):
                q = 3 * p
                pe.wait_ge(s_xg[p], 16 * used + 16)
                for c in range(2):
                    last = m.transpose(bank[PART][:, c * P:(c + 1) * P], xg[:, p, c * P:(c + 1) * P], ident)
                last.then_inc(s_xt, 1)
                pe.wait_ge(s_xgT, e + 1)
                pe.wait_ge(s_slot[q], in_slots[0])
                pe.wait_ge(s_slot[q + 1], in_slots[1])
                for k in range(DK):
                    for g in range(4):
                        w = slot[q + g // 2].rearrange("p (k n) -> p k n", k=DK)
                        last = m.matmul(bank[SUM][32 * g:32 * g + 32, 0:256], xgT[:, k % 2, k // 2], w[:, k, 256 * (g % 2):256 * (g % 2) + 256],
                                        start=k == 0, stop=k == DK - 1)
                last.then_inc(s_gu, 1)
                pe.wait_ge(s_gusb, e + 1)
                for c in range(2):
                    last = m.transpose(bank[QB][:, c * P:(c + 1) * P], gu[:, c * P:(c + 1) * P], ident)
                last.then_inc(s_guT, 1)
                pe.wait_ge(s_hE, e + 1)
                pe.wait_ge(s_slot[q + 2], in_slots[2])
                wd = slot[q + 2].rearrange("p (k n) -> p k n", k=FC)
                for j in range(FC):
                    for g in range(4):
                        last = m.matmul(bank[CHAIN][32 * g:32 * g + 32, 0:256], hE[:, j % 2, j // 2], wd[:, j, 256 * g:256 * g + 256],
                                        start=j == 0, stop=j == FC - 1)
                last.then_inc(s_dn, 1)

            for b, lab in ((QB, ("hT", 1, 0)), (CHAIN, ("blocks",)), (SUM, ("logitsT",)), (PART, ("logits",))):
                pe.wait_ge(*count_taken(*lab))
            with pe.Fori(0, EXPERTS // NB) as i:
                for p in range(NB):
                    expert(NB * i + p, p, i, [16 * i + (SLOT_BASE[3 * p + m] + 16) for m in range(3)])
            for e in range(EXPERTS // NB * NB, EXPERTS):
                p, i = e % NB, e // NB
                expert(e, p, i, [SLOT_BASE[3 * p + m] + 16 * (i + 1) for m in range(3)])
            later_blocks(pe, lambda r: expert(r + EXPERTS, 0, r + FIRST, [16 * r + (AFTER[m] + 16) for m in range(3)]))


_INS = ["x_prompt", "x_sample", "cache_k", "cache_v", "cache_logf", "state_pool", "page_table", "norm_mix", "w_in", "b_forget",
        "w_pool", "pool_scale", "w_up_pool", "w_up_att", "w_out", "norm_ffn", "w_router_group", "b_router_group",
        "w_router_expert", "b_router_expert", "w_gate", "w_up", "w_down", "norm_final"]
_OUTS = [("y_prompt", (1, SEQ, D)), ("y_sample", (NS, 1, D)), ("new_k_prompt", (1, 1, SEQ, HEADS, HD)), ("new_v_prompt", (1, 1, SEQ, HEADS, HD)),
         ("new_logf_prompt", (1, 1, SEQ, HEADS)), ("new_pool_prompt", (1, 1, PLEN, DC)), ("new_k_sample", (1, NS, 1, HEADS, HD)),
         ("new_v_sample", (1, NS, 1, HEADS, HD)), ("new_logf_sample", (1, NS, 1, HEADS)), ("new_pool_sample", (1, NS, PLEN, DC))]


def kernel(**inputs):
    from concourse import bacc
    from concourse.bass_utils import run_bass_kernel_spmd

    early, late, poolc, payload = constants()
    arrays = {name: np.ascontiguousarray(inputs[name]) for name in _INS}
    for name, parts in (("c_early", early), ("c_late", late), ("c_pool", poolc)):
        arrays[name] = np.ascontiguousarray(np.concatenate([np.asarray(a, np.float32) for a in parts.values()], 1))
    arrays["c_pay"] = payload
    nc = bacc.Bacc("TRN2", target_bir_lowering=False, num_devices=1)
    t = {name: nc.dram_tensor(name, a.shape, mybir.dt.from_np(a.dtype), kind="ExternalInput").ap() for name, a in arrays.items()}
    for name, shape in _OUTS:
        t[name] = nc.dram_tensor(name, shape, F32, kind="ExternalOutput").ap()
    build(nc, t)
    r = run_bass_kernel_spmd(nc, [arrays], core_ids=[0])
    return tuple(r.results[0][name] for name, _ in _OUTS)
```
